# Optimizing a Trainium2 kernel written in Bass

```python
import math
import jax, jax.numpy as jnp
from jax import lax
import numpy as np

D_MODEL = 1024
BATCH = 1
SEQ = 512
DEPTH = 1
DEC_BATCH = 8
DEC_SEQ = 1
PAST_LEN = 1024
PAGE_SIZE = 128

HEAD_DIM = 64
N_HEADS = (D_MODEL // 2) // HEAD_DIM
N_KV = 2
Q_PER_KV = N_HEADS // N_KV
ATT_WIDTH = N_HEADS * HEAD_DIM
KV_WIDTH = N_KV * HEAD_DIM
CMP_LEN = 32
CMP_STRIDE = 16
CMP_HIDDEN = HEAD_DIM
SEL_BLOCK = 64
SEL_TOPN = 16
WINDOW = 512
ROPE_THETA = 10000.0
SSM_GROUP = 16
SSM_WIDTH = D_MODEL // 2
SSM_GROUPS = SSM_WIDTH // SSM_GROUP
SSM_STATE = 64
PEER_HEADS = 8
PEER_NKEYS = 128
PEER_EXPERTS = PEER_NKEYS * PEER_NKEYS
PEER_QDIM = 256
PEER_TOPK = 16
PEER_CHUNK = 128
Q_BLOCK = 64
IN_COLS = ATT_WIDTH + 6 * KV_WIDTH + 3 * N_HEADS + SSM_WIDTH + 2 * D_MODEL
RMS_EPS = 1e-6
NEG = -1e30
BIG = 1e9
TINY = 1e-30

kernel_name = 'nsa_s5_peer_hybrid_step'

def _split_points():
    sizes = [ATT_WIDTH] + [KV_WIDTH] * 6 + [3 * N_HEADS, SSM_WIDTH]
    pts, acc = [], 0
    for s in sizes:
        acc += s
        pts.append(acc)
    return pts

def _rmsnorm(x, g):
    xf = x.astype(jnp.float32)
    y = xf * lax.rsqrt(jnp.mean(xf * xf, axis=-1, keepdims=True) + RMS_EPS) * g.astype(jnp.float32)
    return y.astype(x.dtype)

def _rope(x, pos):
    half = HEAD_DIM // 2
    inv = ROPE_THETA ** (-jnp.arange(half, dtype=jnp.float32) / half)
    ang = pos.astype(jnp.float32)[:, None] * inv[None, :]
    cos = jnp.cos(ang)[:, None, :]
    sin = jnp.sin(ang)[:, None, :]
    xf = x.astype(jnp.float32)
    x1, x2 = xf[..., :half], xf[..., half:]
    return jnp.concatenate([x1 * cos - x2 * sin, x2 * cos + x1 * sin], axis=-1).astype(x.dtype)

def _masked_softmax(s, mask):
    s = jnp.where(mask, s, NEG)
    e = jnp.where(mask, jnp.exp(s - jnp.max(s, axis=-1, keepdims=True)), 0.0)
    return e / jnp.maximum(jnp.sum(e, axis=-1, keepdims=True), TINY)

def _compress(k, pe, w1, w2):
    B, L = k.shape[:2]
    lp = -(-L // CMP_STRIDE) * CMP_STRIDE
    k = jnp.pad(k, ((0, 0), (0, lp - L), (0, 0), (0, 0)))
    n_chunk = lp // CMP_STRIDE
    chunks = k.reshape(B, n_chunk, CMP_STRIDE, N_KV, HEAD_DIM)
    r = CMP_LEN // CMP_STRIDE
    nb = n_chunk - r + 1
    hid = None
    for j in range(r):
        wj = w1[j * CMP_STRIDE:(j + 1) * CMP_STRIDE]
        pj = pe[j * CMP_STRIDE:(j + 1) * CMP_STRIDE]
        part = jnp.einsum('bcsgd,sdh->bcgh', chunks, wj)[:, j:j + nb] + jnp.einsum('sd,sdh->h', pj, wj)
        hid = part if hid is None else hid + part
    out = jax.nn.gelu(hid) @ w2
    cend = jnp.arange(nb, dtype=jnp.int32) * CMP_STRIDE + CMP_LEN - 1
    return out, cend

def _cmp_to_sel(nc, ns):
    i = jnp.arange(nc)[:, None]
    j = jnp.arange(ns)[None, :]
    st = i * CMP_STRIDE
    en = st + CMP_LEN - 1
    ss = j * SEL_BLOCK
    se = ss + SEL_BLOCK - 1
    return ((st <= se) & (en >= ss)).astype(jnp.float32)

def _nsa(q, qpos, gates, ck, cv, cend, n_sel_blocks, gather_sel, kwin, vwin, kpos):
    f32 = jnp.float32
    dt = q.dtype
    scale = HEAD_DIM ** -0.5
    s_c = jnp.einsum('bqgrd,bngd->bqgrn', q, ck).astype(f32) * scale
    m_c = (cend[None, :] <= qpos[:, None])[None, :, None, None, :]
    p_c = _masked_softmax(s_c, m_c)
    o_c = jnp.einsum('bqgrn,bngd->bqgrd', p_c.astype(dt), cv)
    imp = jnp.einsum('bqgn,ns->bqgs', jnp.sum(p_c, axis=3), _cmp_to_sel(ck.shape[1], n_sel_blocks))
    j = jnp.arange(n_sel_blocks)[None, :]
    cur = (qpos // SEL_BLOCK)[:, None]
    valid = j * SEL_BLOCK <= qpos[:, None]
    force = (j == 0) | (j == cur) | (j == cur - 1)
    score = jnp.where((valid & force)[None, :, None, :], BIG, jnp.where(valid[None, :, None, :], imp, -BIG))
    _, idx = lax.top_k(score, min(SEL_TOPN, n_sel_blocks))
    k_s, v_s, p_s = gather_sel(idx)
    s_s = jnp.einsum('bqgrd,bqgkd->bqgrk', q, k_s).astype(f32) * scale
    m_s = (p_s <= qpos[None, :, None, None])[:, :, :, None, :]
    o_s = jnp.einsum('bqgrk,bqgkd->bqgrd', _masked_softmax(s_s, m_s).astype(dt), v_s)
    s_w = jnp.einsum('bqgrd,bkgd->bqgrk', q, kwin).astype(f32) * scale
    dlt = qpos[:, None] - kpos[None, :]
    m_w = ((kpos[None, :] >= 0) & (dlt >= 0) & (dlt < WINDOW))[None, :, None, None, :]
    o_w = jnp.einsum('bqgrk,bkgd->bqgrd', _masked_softmax(s_w, m_w).astype(dt), vwin)
    g = jax.nn.sigmoid(gates.astype(f32))
    o = g[..., 0:1] * o_c + g[..., 1:2] * o_s + g[..., 2:3] * o_w
    B, Q = q.shape[:2]
    return o.reshape(B, Q, ATT_WIDTH).astype(dt)

def _scan_combine(e1, e2):
    a1, b1 = e1
    a2, b2 = e2
    return a1 * a2, a2 * b1 + b2

def _ssm(u, h0, lp):
    f32 = jnp.float32
    B, T = u.shape[:2]
    uf = u.reshape(B, T, SSM_GROUPS, SSM_GROUP).astype(f32)
    lam = lax.complex(lp['ssm_a_re'].astype(f32), lp['ssm_a_im'].astype(f32))
    step = jnp.exp(lp['ssm_log_dt'].astype(f32))[:, None]
    a_bar = jnp.exp(lam * step)
    b_bar = ((a_bar - 1.0) / lam)[..., None] * lax.complex(lp['ssm_b_re'].astype(f32), lp['ssm_b_im'].astype(f32))
    c = lax.complex(lp['ssm_c_re'].astype(f32), lp['ssm_c_im'].astype(f32))
    bu = jnp.einsum('gpc,btgc->btgp', b_bar, uf.astype(jnp.complex64))
    bu = bu.at[:, 0].add(a_bar * h0)
    a_seq = jnp.broadcast_to(a_bar, bu.shape)
    _, hs = lax.associative_scan(_scan_combine, (a_seq, bu), axis=1)
    y = jnp.real(jnp.einsum('gcp,btgp->btgc', c, hs)) + lp['ssm_d'].astype(f32) * uf
    return y.reshape(B, T, SSM_WIDTH), hs[:, -1]

def _merge(o_att, y_ssm, g_mrg, lp):
    dt = o_att.dtype
    a = o_att @ lp['w_att_proj']
    gl = jax.nn.gelu(y_ssm).astype(dt) @ lp['w_ssm_glu']
    s = gl[..., :D_MODEL] * jax.nn.sigmoid(gl[..., D_MODEL:])
    m = jax.nn.sigmoid(g_mrg[..., :D_MODEL]) * a + jax.nn.sigmoid(g_mrg[..., D_MODEL:]) * s
    return m @ lp['w_out']

def _project(h, lp, pos):
    B, T, _ = h.shape
    z = h @ lp['w_in']
    q, kc, vc, ks, vs, kw, vw, g_nsa, u, g_mrg = jnp.split(z, _split_points(), axis=-1)
    kv = lambda t: t.reshape(B, T, N_KV, HEAD_DIM)
    q = _rope(q.reshape(B, T, N_HEADS, HEAD_DIM), pos).reshape(B, T, N_KV, Q_PER_KV, HEAD_DIM)
    return (q, _rope(kv(kc), pos), kv(vc), _rope(kv(ks), pos), kv(vs), _rope(kv(kw), pos), kv(vw),
            g_nsa.reshape(B, T, N_KV, Q_PER_KV, 3), u, g_mrg)

def _mix_prompt(h, lp):
    B, T, _ = h.shape
    pos = jnp.arange(T, dtype=jnp.int32)
    q, kc, vc, ks, vs, kw, vw, gates, u, g_mrg = _project(h, lp, pos)
    ck, cend = _compress(kc, lp['cmp_pe_k'], lp['cmp_w1_k'], lp['cmp_w2_k'])
    cv, _ = _compress(vc, lp['cmp_pe_v'], lp['cmp_w1_v'], lp['cmp_w2_v'])
    ns = -(-T // SEL_BLOCK)
    bi = jnp.arange(B)[:, None, None, None, None]
    gi = jnp.arange(N_KV)[None, None, :, None, None]

    def gather_sel(idx):
        p = idx[..., None] * SEL_BLOCK + jnp.arange(SEL_BLOCK)
        pc = jnp.minimum(p, T - 1)
        Q, K = idx.shape[1], idx.shape[3] * SEL_BLOCK
        return (ks[bi, pc, gi].reshape(B, Q, N_KV, K, HEAD_DIM),
                vs[bi, pc, gi].reshape(B, Q, N_KV, K, HEAD_DIM),
                p.reshape(B, Q, N_KV, K))

    kw_pad = jnp.pad(kw, ((0, 0), (WINDOW, 0), (0, 0), (0, 0)))
    vw_pad = jnp.pad(vw, ((0, 0), (WINDOW, 0), (0, 0), (0, 0)))
    nqb = T // Q_BLOCK
    q_blk = jnp.swapaxes(q.reshape(B, nqb, Q_BLOCK, N_KV, Q_PER_KV, HEAD_DIM), 0, 1)
    g_blk = jnp.swapaxes(gates.reshape(B, nqb, Q_BLOCK, N_KV, Q_PER_KV, 3), 0, 1)
    starts = jnp.arange(nqb, dtype=jnp.int32) * Q_BLOCK

    def one_block(args):
        qb, gb, s = args
        qpos = s + jnp.arange(Q_BLOCK, dtype=jnp.int32)
        kwin = lax.dynamic_slice_in_dim(kw_pad, s, Q_BLOCK + WINDOW, axis=1)
        vwin = lax.dynamic_slice_in_dim(vw_pad, s, Q_BLOCK + WINDOW, axis=1)
        kpos = s - WINDOW + jnp.arange(Q_BLOCK + WINDOW, dtype=jnp.int32)
        return _nsa(qb, qpos, gb, ck, cv, cend, ns, gather_sel, kwin, vwin, kpos)

    o = lax.map(one_block, (q_blk, g_blk, starts))
    o = jnp.swapaxes(o, 0, 1).reshape(B, T, ATT_WIDTH)
    h0 = jnp.zeros((B, SSM_GROUPS, SSM_STATE), jnp.complex64)
    y_ssm, h_last = _ssm(u, h0, lp)
    out = _merge(o, y_ssm, g_mrg, lp)
    wb = min(WINDOW, T)
    new = (kc, vc, ks, vs, kw[:, T - wb:], vw[:, T - wb:], jnp.real(h_last), jnp.imag(h_last))
    return out, new

def _mix_sample(h, ckp, cvp, ksp, vsp, kwb, vwb, s_re, s_im, page_table, lp):
    DB, S, _ = h.shape
    n_pages = page_table.shape[1]
    past = n_pages * PAGE_SIZE
    pos = past + jnp.arange(S, dtype=jnp.int32)
    q, kc, vc, ks, vs, kw, vw, gates, u, g_mrg = _project(h, lp, pos)
    full_kc = jnp.concatenate([ckp[page_table].reshape(DB, past, N_KV, HEAD_DIM), kc], axis=1)
    full_vc = jnp.concatenate([cvp[page_table].reshape(DB, past, N_KV, HEAD_DIM), vc], axis=1)
    ck, cend = _compress(full_kc, lp['cmp_pe_k'], lp['cmp_w1_k'], lp['cmp_w2_k'])
    cv, _ = _compress(full_vc, lp['cmp_pe_v'], lp['cmp_w1_v'], lp['cmp_w2_v'])
    ns = -(-(past + S) // SEL_BLOCK)
    bi = jnp.arange(DB)[:, None, None, None, None]
    gi = jnp.arange(N_KV)[None, None, :, None, None]

    def gather_sel(idx):
        p = idx[..., None] * SEL_BLOCK + jnp.arange(SEL_BLOCK)
        is_past = (p < past)[..., None]
        pp = jnp.clip(p, 0, past - 1)
        page = page_table[bi, pp // PAGE_SIZE]
        off = pp % PAGE_SIZE
        pn = jnp.clip(p - past, 0, S - 1)
        Q, K = idx.shape[1], idx.shape[3] * SEL_BLOCK
        kk = jnp.where(is_past, ksp[page, off, gi], ks[bi, pn, gi])
        vv = jnp.where(is_past, vsp[page, off, gi], vs[bi, pn, gi])
        return (kk.reshape(DB, Q, N_KV, K, HEAD_DIM), vv.reshape(DB, Q, N_KV, K, HEAD_DIM),
                p.reshape(DB, Q, N_KV, K))

    wbuf = kwb.shape[1]
    kwin = jnp.concatenate([kwb, kw], axis=1)
    vwin = jnp.concatenate([vwb, vw], axis=1)
    kpos = past - wbuf + jnp.arange(wbuf + S, dtype=jnp.int32)
    o = _nsa(q, pos, gates, ck, cv, cend, ns, gather_sel, kwin, vwin, kpos)
    h0 = lax.complex(s_re.astype(jnp.float32), s_im.astype(jnp.float32))
    y_ssm, h_last = _ssm(u, h0, lp)
    out = _merge(o, y_ssm, g_mrg, lp)
    nw = min(WINDOW, wbuf + S)
    new = (kc, vc, ks, vs, kwin[:, wbuf + S - nw:], vwin[:, wbuf + S - nw:], jnp.real(h_last), jnp.imag(h_last))
    return out, new

def _peer(h, w_q, k1, k2, u_tab, v_tab):
    shp = h.shape
    hf = h.reshape(-1, D_MODEL)
    n = hf.shape[0]
    n_pad = -(-n // PEER_CHUNK) * PEER_CHUNK
    hf = jnp.pad(hf, ((0, n_pad - n), (0, 0))).reshape(n_pad // PEER_CHUNK, PEER_CHUNK, D_MODEL)
    half = PEER_QDIM // 2

    def one(hc):
        q = (hc @ w_q).reshape(PEER_CHUNK, PEER_HEADS, PEER_QDIM)
        s1 = jnp.einsum('nhd,kd->nhk', q[..., :half], k1).astype(jnp.float32)
        s2 = jnp.einsum('nhd,kd->nhk', q[..., half:], k2).astype(jnp.float32)
        v1, i1 = lax.top_k(s1, PEER_TOPK)
        v2, i2 = lax.top_k(s2, PEER_TOPK)
        cand = (v1[..., :, None] + v2[..., None, :]).reshape(PEER_CHUNK, PEER_HEADS, PEER_TOPK * PEER_TOPK)
        sc, ci = lax.top_k(cand, PEER_TOPK)
        e = (jnp.take_along_axis(i1, ci // PEER_TOPK, axis=-1) * PEER_NKEYS
             + jnp.take_along_axis(i2, ci % PEER_TOPK, axis=-1))
        g = jax.nn.softmax(sc, axis=-1)
        act = jax.nn.gelu(jnp.einsum('nhkd,nd->nhk', u_tab[e], hc).astype(jnp.float32))
        return jnp.einsum('nhk,nhkd->nd', (g * act).astype(hc.dtype), v_tab[e])

    out = lax.map(one, hf).reshape(n_pad, D_MODEL)[:n]
    return out.reshape(shp)

def setup_inputs(seed: int = 0) -> dict:
    key = jax.random.key(seed)
    ks = jax.random.split(key, 40)
    f32 = jnp.float32
    nrm = lambda k, shape, s: jax.random.normal(k, shape, f32) * s
    n_pages = PAST_LEN // PAGE_SIZE
    n_pool = (5 * DEC_BATCH * n_pages) // 4
    wbuf = min(WINDOW, PAST_LEN)
    pool = (DEPTH, n_pool, PAGE_SIZE, N_KV, HEAD_DIM)
    win = (DEPTH, DEC_BATCH, wbuf, N_KV, HEAD_DIM)
    st = (DEPTH, DEC_BATCH, SSM_GROUPS, SSM_STATE)
    page_table = jax.random.permutation(ks[10], n_pool)[:DEC_BATCH * n_pages].reshape(DEC_BATCH, n_pages).astype(jnp.int32)
    a_im = jnp.broadcast_to(math.pi * jnp.arange(SSM_STATE, dtype=f32), (DEPTH, SSM_GROUPS, SSM_STATE))
    return {
        'x_prompt': nrm(ks[0], (BATCH, SEQ, D_MODEL), 1.0),
        'x_sample': nrm(ks[1], (DEC_BATCH, DEC_SEQ, D_MODEL), 1.0),
        'cache_k_cmp': nrm(ks[2], pool, 1.0),
        'cache_v_cmp': nrm(ks[3], pool, 1.0),
        'cache_k_sel': nrm(ks[4], pool, 1.0),
        'cache_v_sel': nrm(ks[5], pool, 1.0),
        'cache_k_win': nrm(ks[6], win, 1.0),
        'cache_v_win': nrm(ks[7], win, 1.0),
        'state_ssm_re': nrm(ks[8], st, 0.1),
        'state_ssm_im': nrm(ks[9], st, 0.1),
        'page_table': page_table,
        'norm_mix': 1.0 + nrm(ks[11], (DEPTH, D_MODEL), 0.01),
        'w_in': nrm(ks[12], (DEPTH, D_MODEL, IN_COLS), D_MODEL ** -0.5),
        'cmp_pe_k': nrm(ks[13], (DEPTH, CMP_LEN, HEAD_DIM), 0.1),
        'cmp_w1_k': nrm(ks[14], (DEPTH, CMP_LEN, HEAD_DIM, CMP_HIDDEN), (CMP_LEN * HEAD_DIM) ** -0.5),
        'cmp_w2_k': nrm(ks[15], (DEPTH, CMP_HIDDEN, HEAD_DIM), CMP_HIDDEN ** -0.5),
        'cmp_pe_v': nrm(ks[16], (DEPTH, CMP_LEN, HEAD_DIM), 0.1),
        'cmp_w1_v': nrm(ks[17], (DEPTH, CMP_LEN, HEAD_DIM, CMP_HIDDEN), (CMP_LEN * HEAD_DIM) ** -0.5),
        'cmp_w2_v': nrm(ks[18], (DEPTH, CMP_HIDDEN, HEAD_DIM), CMP_HIDDEN ** -0.5),
        'ssm_a_re': -0.5 + nrm(ks[19], (DEPTH, SSM_GROUPS, SSM_STATE), 0.01),
        'ssm_a_im': a_im + nrm(ks[20], (DEPTH, SSM_GROUPS, SSM_STATE), 0.01),
        'ssm_log_dt': jax.random.uniform(ks[21], (DEPTH, SSM_GROUPS), f32, math.log(0.001), math.log(0.1)),
        'ssm_b_re': nrm(ks[22], (DEPTH, SSM_GROUPS, SSM_STATE, SSM_GROUP), (2 * SSM_GROUP) ** -0.5),
        'ssm_b_im': nrm(ks[23], (DEPTH, SSM_GROUPS, SSM_STATE, SSM_GROUP), (2 * SSM_GROUP) ** -0.5),
        'ssm_c_re': nrm(ks[24], (DEPTH, SSM_GROUPS, SSM_GROUP, SSM_STATE), (2 * SSM_STATE) ** -0.5),
        'ssm_c_im': nrm(ks[25], (DEPTH, SSM_GROUPS, SSM_GROUP, SSM_STATE), (2 * SSM_STATE) ** -0.5),
        'ssm_d': nrm(ks[26], (DEPTH, SSM_GROUPS, SSM_GROUP), 1.0),
        'w_att_proj': nrm(ks[27], (DEPTH, ATT_WIDTH, D_MODEL), ATT_WIDTH ** -0.5),
        'w_ssm_glu': nrm(ks[28], (DEPTH, SSM_WIDTH, 2 * D_MODEL), SSM_WIDTH ** -0.5),
        'w_out': nrm(ks[29], (DEPTH, D_MODEL, D_MODEL), D_MODEL ** -0.5),
        'norm_ffn': 1.0 + nrm(ks[30], (DEPTH, D_MODEL), 0.01),
        'peer_w_q': nrm(ks[31], (DEPTH, D_MODEL, PEER_HEADS * PEER_QDIM), D_MODEL ** -0.5),
        'peer_keys1': nrm(ks[32], (DEPTH, PEER_NKEYS, PEER_QDIM // 2), (PEER_QDIM // 2) ** -0.5),
        'peer_keys2': nrm(ks[33], (DEPTH, PEER_NKEYS, PEER_QDIM // 2), (PEER_QDIM // 2) ** -0.5),
        'peer_u': nrm(ks[34], (DEPTH, PEER_EXPERTS, D_MODEL), D_MODEL ** -0.5),
        'peer_v': nrm(ks[35], (DEPTH, PEER_EXPERTS, D_MODEL), PEER_HEADS ** -0.5),
        'norm_final': 1.0 + nrm(ks[36], (D_MODEL,), 0.01),
    }

def reference(x_prompt, x_sample, cache_k_cmp, cache_v_cmp, cache_k_sel, cache_v_sel, cache_k_win, cache_v_win,
              state_ssm_re, state_ssm_im, page_table, norm_mix, w_in, cmp_pe_k, cmp_w1_k, cmp_w2_k,
              cmp_pe_v, cmp_w1_v, cmp_w2_v, ssm_a_re, ssm_a_im, ssm_log_dt, ssm_b_re, ssm_b_im, ssm_c_re,
              ssm_c_im, ssm_d, w_att_proj, w_ssm_glu, w_out, norm_ffn, peer_w_q, peer_keys1, peer_keys2,
              peer_u, peer_v, norm_final):
    yp, ys = x_prompt, x_sample
    sp, ss = [], []
    for l in range(DEPTH):
        lp = {'w_in': w_in[l], 'cmp_pe_k': cmp_pe_k[l], 'cmp_w1_k': cmp_w1_k[l], 'cmp_w2_k': cmp_w2_k[l],
              'cmp_pe_v': cmp_pe_v[l], 'cmp_w1_v': cmp_w1_v[l], 'cmp_w2_v': cmp_w2_v[l],
              'ssm_a_re': ssm_a_re[l], 'ssm_a_im': ssm_a_im[l], 'ssm_log_dt': ssm_log_dt[l],
              'ssm_b_re': ssm_b_re[l], 'ssm_b_im': ssm_b_im[l], 'ssm_c_re': ssm_c_re[l], 'ssm_c_im': ssm_c_im[l],
              'ssm_d': ssm_d[l], 'w_att_proj': w_att_proj[l], 'w_ssm_glu': w_ssm_glu[l], 'w_out': w_out[l]}
        mp, st_p = _mix_prompt(_rmsnorm(yp, norm_mix[l]), lp)
        ms, st_s = _mix_sample(_rmsnorm(ys, norm_mix[l]), cache_k_cmp[l], cache_v_cmp[l], cache_k_sel[l],
                               cache_v_sel[l], cache_k_win[l], cache_v_win[l], state_ssm_re[l], state_ssm_im[l],
                               page_table, lp)
        yp = yp + mp
        ys = ys + ms
        yp = yp + _peer(_rmsnorm(yp, norm_ffn[l]), peer_w_q[l], peer_keys1[l], peer_keys2[l], peer_u[l], peer_v[l])
        ys = ys + _peer(_rmsnorm(ys, norm_ffn[l]), peer_w_q[l], peer_keys1[l], peer_keys2[l], peer_u[l], peer_v[l])
        sp.append(st_p)
        ss.append(st_s)
    y_prompt = _rmsnorm(yp, norm_final)
    y_sample = _rmsnorm(ys, norm_final)
    stk = lambda lst, i: jnp.stack([t[i] for t in lst])
    p_k_cmp, p_v_cmp, p_k_sel, p_v_sel = stk(sp, 0), stk(sp, 1), stk(sp, 2), stk(sp, 3)
    p_k_win, p_v_win, p_ssm_re, p_ssm_im = stk(sp, 4), stk(sp, 5), stk(sp, 6), stk(sp, 7)
    s_k_cmp, s_v_cmp, s_k_sel, s_v_sel = stk(ss, 0), stk(ss, 1), stk(ss, 2), stk(ss, 3)
    s_k_win, s_v_win, s_ssm_re, s_ssm_im = stk(ss, 4), stk(ss, 5), stk(ss, 6), stk(ss, 7)
    return (y_prompt, y_sample, p_k_cmp, p_v_cmp, p_k_sel, p_v_sel, p_k_win, p_v_win, p_ssm_re, p_ssm_im,
            s_k_cmp, s_v_cmp, s_k_sel, s_v_sel, s_k_win, s_v_win, s_ssm_re, s_ssm_im)


_drawn_inputs = setup_inputs


def setup_inputs(seed=0):
    import zlib

    import numpy as np

    out = dict(_drawn_inputs(seed))
    spreads = {}
    factors = {'norm_mix': 5.202,
     'cmp_pe_k': 6.81,
     'ssm_a_re': 17.136,
     'norm_ffn': 11.742,
     'norm_final': 28.505,
     'cmp_pe_v': 3.701,
     'ssm_c_re': 2.897,
     'ssm_c_im': 3.472}
    for name, (base, spread) in spreads.items():
        noise = np.random.default_rng([zlib.crc32(name.encode()), seed]).standard_normal(out[name].shape)
        drawn = base * np.exp(spread * noise) if base else spread * noise
        out[name] = __import__('jax').numpy.asarray(drawn.astype(out[name].dtype))
    for name, factor in factors.items():
        out[name] = (out[name] * factor).astype(out[name].dtype)
    return out
```

```python
import math
from contextlib import ExitStack

import numpy as np

import concourse.bass as bass
from concourse import mybir

ALU = mybir.AluOpType
ACT = mybir.ActivationFunctionType
AX_X = mybir.AxisListType.X
F32 = mybir.dt.float32
BF16 = mybir.dt.bfloat16
I32 = mybir.dt.int32
U32 = mybir.dt.uint32

P = 128
D = 1024
KT = D // P
SEQ = 512
NB = 8
PAST = 1024
PAGE = 128
NPG = PAST // PAGE
TOK = SEQ + NB
HALF = TOK // 2
TILES = 5
PAD = TILES * P
HD = 64
NH = 8
NKV = 2
REP = NH // NKV
KVW = NKV * HD
NAT = NH * HD + 6 * KVW + 3 * NH
C_K = NH * HD
C_GATE = C_K + 6 * KVW
EPS = 1e-6
NEG = -1e30
TINY = 1e-30
SCALE = HD ** -0.5
CHUNK = 512
CMP_LEN, CMP_STRIDE = 32, 16
NC_P = SEQ // CMP_STRIDE - 1
NC_S = PAST // CMP_STRIDE - 1
SEL_BLOCK = 64
NS_S = PAST // SEL_BLOCK + 1
NT_ST = 16
STATE = 64
GRP_CH = 16
HEADS_P = 8
NKEYS = 128
TOPK = 16
HK = HEADS_P * TOPK
LOW = -3.0e38


def rows(t):
    return P if t < SEQ // P else NB


def new_semaphore(nc, ctx, sems, name):
    if not sems:
        nc.reset_free_semaphores(sorted(nc.free_semaphores))
    sems.append(ctx.enter_context(nc.semaphore(name)))
    return sems[-1]


def open_block(nc, ctx, sems):
    numbers = sorted(s.num for s in sems)
    assert numbers == list(range(numbers[0], numbers[0] + len(numbers)))
    ctx.callback(lambda: nc.all_engine_barrier(sems_to_clear=range(numbers[0], numbers[-1] + 1)))
    return ctx.enter_context(nc.Block())


def own(engine, sem):
    count = [0]

    def link(ins):
        count[0] += 1
        ins.then_inc(sem, 1)
        engine.wait_ge(sem, count[0])
    return link


def norm_tile(dve, link, t, out, x, gain, ss, rstd, sq_done, var_ready, root_ready, normed):
    r = rstd[:, t:t + 1]
    dve.wait_ge(sq_done, t + 1)
    dve.tensor_scalar(r, ss[:, t:t + 1], 1.0 / D, EPS, ALU.mult, ALU.add).then_inc(var_ready, 1)
    dve.wait_ge(root_ready, t + 1)
    link(dve.reciprocal(r, r))
    dve.scalar_tensor_tensor(out=out[:, t, :], in0=x[:, t, :], scalar=r, in1=gain[:],
                             op0=ALU.mult, op1=ALU.mult).then_inc(normed, 1)


def square_tile(act, t, x, junk, ss, rstd, sq_done, var_ready, root_ready):
    act.activation(junk[:], x[:, t, :], ACT.Square, accum_out=ss[:, t:t + 1]).then_inc(sq_done, 1)
    act.wait_ge(var_ready, t + 1)
    act.activation(rstd[:, t:t + 1], rstd[:, t:t + 1], ACT.Sqrt).then_inc(root_ready, 1)


def stage_project(nc, io, S):
    with ExitStack() as ctx:
        sb = lambda n, s, d=F32: ctx.enter_context(nc.sbuf_tensor("pr_" + n, s, d))
        sems = []
        sem = lambda n: new_semaphore(nc, ctx, sems, n)
        x = sb("x", [P, TILES, D])
        gain = sb("gain", [P, D])
        junk = sb("junk", [P, D])
        ss = sb("ss", [P, TILES])
        rstd = sb("rstd", [P, TILES])
        hT = sb("hT", [P, KT, PAD])
        ring = sb("ring", [P, 3, KT, CHUNK])
        ps = [ctx.enter_context(nc.psum_tensor(f"pz{i}", [P, CHUNK], F32)) for i in range(6)]
        pt = [ctx.enter_context(nc.psum_tensor(f"pt{i}", [P, CHUNK], F32)) for i in range(2)]
        pads_zero, ident_ready = sem("pads_zero"), sem("ident_ready")
        x_landed = sem("x_landed")
        xt_landed = [sem(f"xt_landed{t}") for t in range(TILES)]
        w_landed = [sem(f"w_landed{i}") for i in range(3)]
        sq_done, var_ready, root_ready, normed = sem("sq_done"), sem("var_ready"), sem("root_ready"), sem("normed")
        dve_own = sem("dve_own")
        tr_done, hT_ready, z_done, z_kept = sem("tr_done"), sem("hT_ready"), sem("z_done"), sem("z_kept")
        w_in = io["w_in"].rearrange("a (k p) n -> p (a k) n", p=P)
        w_heads = io["w_in_heads"].rearrange("(k p) n -> p k n", p=P)

        chunks = [(0, 512, "z"), (512, 512, "z"), (1024, NAT - 1024, "z"), (NAT, 512, "u")]
        chunks += [(NAT + 512 + CHUNK * j, CHUNK, "g") for j in range(4)]
        groups = []
        for c, (c0, n, what) in enumerate(chunks):
            if what == "z":
                groups += [(c, t, None) for t in range(TILES)]
            else:
                groups += [(c, m, h) for m in range(4) for h in range(2)]
        ends = [sum(g[0] <= c for g in groups) for c in range(len(chunks))]
        block = open_block(nc, ctx, sems)

        @block.gpsimd
        def _(pool):
            pool.memset(x[:, 4, :], 0.0).then_inc(pads_zero, 1)
            pool.memset(S.ident[:], 0.0).then_inc(ident_ready, 1)
            pool.wait_ge(ident_ready, 1)
            pool.affine_select(out=S.ident[:], in_=S.ident[:], compare_op=ALU.not_equal, fill=1.0, base=0,
                               pattern=[[-1, P]], channel_multiplier=1).then_inc(ident_ready, 1)

        @block.sync
        def _(sp):
            for t in range(4):
                sp.dma_start(x[:, t, :], io["x_prompt"][0, P * t:P * t + P, :]).then_inc(xt_landed[t], 16)
                if t == 0:
                    sp.dma_start(gain[:], io["norm_mix"][0, :].partition_broadcast(P)).then_inc(x_landed, 16)
            sp.wait_ge(pads_zero, 1)
            sp.dma_start(x[0:NB, 4, :], io["x_sample"].rearrange("b a n -> (b a) n")).then_inc(xt_landed[4], 16)
            for c, (c0, n, _w) in enumerate(chunks):
                if c >= 3:
                    sp.wait_ge(z_done, ends[c - 3])
                src = w_heads if c == 0 else w_in[:, :, c0:c0 + n]
                sp.dma_start(ring[:, c % 3, :, 0:n], src).then_inc(w_landed[c % 3], 16)

        @block.vector
        def _(dve):
            link = own(dve, dve_own)
            dve.wait_ge(x_landed, 16)
            for t in range(TILES):
                norm_tile(dve, link, t, x, x, gain, ss, rstd, sq_done, var_ready, root_ready, normed)

        @block.scalar
        def _(act):
            for j in range(2 * TILES):
                t, kh = divmod(j, 2)
                if kh == 0:
                    act.wait_ge(xt_landed[t], 16)
                    square_tile(act, t, x, junk, ss, rstd, sq_done, var_ready, root_ready)
                act.wait_ge(tr_done, j + 1)
                act.activation(hT[:, 4 * kh:4 * kh + 4, P * t:P * t + P],
                               pt[j % 2][:].rearrange("p (k n) -> p k n", k=4), ACT.Copy).then_inc(hT_ready, 1)
            for j, (c, m, h) in enumerate(groups):
                c0, n, what = chunks[c]
                act.wait_ge(z_done, j + 1)
                if what == "z":
                    act.activation(S.z[:, m, c0:c0 + n], ps[j % 6][:, 0:n], ACT.Copy).then_inc(z_kept, 1)
                elif what == "u":
                    act.activation(S.uT[:, m, HALF * h:HALF * h + HALF], ps[j % 6][:, 0:HALF],
                                   ACT.Copy).then_inc(z_kept, 1)
                else:
                    act.activation(S.sgT[:, 4 * (c - 4) + m, HALF * h:HALF * h + HALF], ps[j % 6][:, 0:HALF],
                                   ACT.Sigmoid).then_inc(z_kept, 1)

        @block.tensor
        def _(pe):
            pe.wait_ge(ident_ready, 2)
            for j in range(2 * TILES):
                t, kh = divmod(j, 2)
                pe.wait_ge(normed, t + 1)
                if j >= 2:
                    pe.wait_ge(hT_ready, j - 1)
                for k in range(4):
                    last = pe.transpose(pt[j % 2][:, P * k:P * k + P], x[:, t, P * (4 * kh + k):P * (4 * kh + k) + P],
                                        S.ident[:])
                last.then_inc(tr_done, 1)
            pe.wait_ge(hT_ready, 2 * TILES)
            at = -1
            for j, (c, m, h) in enumerate(groups):
                c0, n, what = chunks[c]
                if c != at:
                    pe.wait_ge(w_landed[c % 3], 16 * (c // 3 + 1))
                    at = c
                if j >= 6:
                    pe.wait_ge(z_kept, j - 5)
                for k in range(KT):
                    if what == "z":
                        last = pe.matmul(ps[j % 6][:, 0:n], hT[:, k, P * m:P * m + P], ring[:, c % 3, k, 0:n],
                                         start=(k == 0), stop=(k == KT - 1))
                    else:
                        last = pe.matmul(ps[j % 6][:, 0:HALF], ring[:, c % 3, k, P * m:P * m + P],
                                         hT[:, k, HALF * h:HALF * h + HALF], start=(k == 0), stop=(k == KT - 1))
                last.then_inc(z_done, 1)


def stage_attend(nc, io, S):
    assert SEQ // SEL_BLOCK <= 16 and SEQ <= 512
    NQ = SEQ // P
    UNITS = [(i, h) for i in range(NQ) for h in range(NH)]
    with ExitStack() as ctx:
        sb = lambda n, s, d=F32: ctx.enter_context(nc.sbuf_tensor("at_" + n, s, d))
        sems = []
        sem = lambda n: new_semaphore(nc, ctx, sems, n)
        cos = sb("cos", [P, TILES, HD // 2])
        sin = sb("sin", [P, TILES, HD // 2])
        prod = sb("prod", [P, 4, TILES * NH * HD // 2])
        qT = sb("qT", [P, REP, PAD])
        xT = sb("xT", [P, 4, PAD])
        causal = sb("causal", [P, P])
        cneg = sb("cneg", [P, NQ, NC_P])
        c01 = sb("c01", [P, NQ, NC_P])
        hid = sb("hid", [NC_P + 2, 2, P])
        gh = sb("gh", [P, 2, NC_P])
        ckT = sb("ckT", [P, NKV, NC_P])
        cv = sb("cv", [NC_P, KVW])
        pc = sb("pc", [P, NQ, NH, NC_P])
        pcT = sb("pcT", [NC_P, NH * P])
        cmx = sb("cmx", [P, NQ, NH])
        csum = sb("csum", [P, NQ, NH])
        prob = sb("prob", [P, 2, 2, SEQ])
        probT = sb("probT", [P, 2, 2, SEQ])
        nmax = sb("nmax", [P, 2, 2])
        psum_row = sb("psum_row", [P, 2, 2])
        coef = sb("coef", [P, 2, 2])
        o = sb("o", [P, NQ, NH * HD])
        sc = ctx.enter_context(nc.psum_tensor("sc", [P, 4, 512], F32))
        tp = ctx.enter_context(nc.psum_tensor("tp", [P, 2, 512], F32))
        oo = ctx.enter_context(nc.psum_tensor("oo", [P, 2, 512], F32))
        names = ("tables", "w_cmp", "masks", "zeroed", "roped", "rope_own", "tr_done", "tr_kept", "hid_done", "bias_kept",
                 "hid_kept", "hidT_done", "gh_ready", "cmp_done", "cmp_kept", "csc_done", "cmx_ready", "cexp_ready", "coefc_ready", "ct_done",
                 "ct_kept", "cpv_done", "ocmp_ready", "s_done", "max_ready", "p_ready", "t_done", "pt0", "pt1",
                 "pv_done", "o_done", "ot_done", "ot_kept", "stored", "gates_ready", "small_kept", "ck_zero")
        E = {n: sem("at_" + n) for n in names}
        z = S.z
        gates = S.gates

        def head(h):
            return (h // REP) * HD, h % REP

        def gate(h):
            return 3 * (h % REP * NKV + h // REP)

        block = open_block(nc, ctx, sems)

        @block.gpsimd
        def _(pool):
            for w in (S.w1k, S.w1v, S.w2k, S.w2v):
                pool.memset(w[:], 0.0).then_inc(E["zeroed"], 1)
            pool.memset(ckT[:], 0.0).then_inc(E["ck_zero"], 1)
            pool.memset(causal[:], 0.0).then_inc(E["masks"], 1)
            pool.memset(cneg[:], 0.0).then_inc(E["masks"], 1)
            pool.memset(c01[:], 1.0).then_inc(E["masks"], 1)
            pool.wait_ge(E["masks"], 3)
            pool.affine_select(out=causal[:], in_=causal[:], pattern=[[-1, P]], compare_op=ALU.is_ge, fill=NEG,
                               base=0, channel_multiplier=1).then_inc(E["masks"], 1)
            for m, fill in ((cneg, NEG), (c01, 0.0)):
                pool.affine_select(out=m[:], in_=m[:], pattern=[[P, NQ], [-CMP_STRIDE, NC_P]], compare_op=ALU.is_ge,
                                   fill=fill, base=1 - CMP_LEN, channel_multiplier=1).then_inc(E["masks"], 1)

        @block.sync
        def _(sp):
            sp.dma_start(cos[:], io["rope_cos"]).then_inc(E["tables"], 16)
            sp.dma_start(sin[:], io["rope_sin"]).then_inc(E["tables"], 16)
            sp.wait_ge(E["zeroed"], 4)
            for w, src in ((S.w1k, "cmp_w1_k"), (S.w1v, "cmp_w1_v")):
                for g in range(NKV):
                    sp.dma_start(w[HD * g:HD * g + HD, :, HD * g:HD * g + HD],
                                 io[src].rearrange("a s d h -> d (a s) h")).then_inc(E["w_cmp"], 16)
            for w, src in ((S.w2k, "cmp_w2_k"), (S.w2v, "cmp_w2_v")):
                for g in range(NKV):
                    sp.dma_start(w[HD * g:HD * g + HD, HD * g:HD * g + HD],
                                 io[src].rearrange("a d h -> d (a h)")).then_inc(E["w_cmp"], 16)
            for j, src in enumerate(("peT_k", "peT_v")):
                for g in range(NKV):
                    sp.dma_start(xT[HD * g:HD * g + HD, j, SEQ:SEQ + CMP_LEN], io[src]).then_inc(E["w_cmp"], 16)
            n = 0
            for b, (name, k) in enumerate((("v_cmp", 1), ("v_sel", 3), ("v_win", 5), ("k_cmp", 0), ("k_sel", 2), ("k_win", 4))):
                if b >= 3:
                    sp.wait_ge(E["roped"], 2 + b - 3)
                c = C_K + KVW * k
                sp.dma_start(io["p_" + name].rearrange("a b (t p) g d -> p (a b t) (g d)", p=P),
                             z[:, 0:NQ, c:c + KVW]).then_inc(E["stored"], 16)
                n += 1
                to = io["s_" + name]
                if name[2:] == "win":
                    old = io["cache_" + name]
                    w = old.shape[2]
                    sp.dma_start(to[0, :, 0:w - 1].rearrange("b w g d -> b (w g d)"),
                                 old[0, :, 1:w].rearrange("b w g d -> b (w g d)")).then_inc(E["stored"], 16)
                    sp.dma_start(to[0, :, w - 1].rearrange("b g d -> b (g d)"), z[0:NB, 4, c:c + KVW]).then_inc(E["stored"], 16)
                    n += 2
                else:
                    sp.dma_start(to.rearrange("a b s g d -> b (a s g d)"), z[0:NB, 4, c:c + KVW]).then_inc(E["stored"], 16)
                    n += 1
            sp.wait_ge(E["stored"], 16 * n)

        @block.vector
        def _(dve):
            link = own(dve, E["rope_own"])
            dve.wait_ge(E["tables"], 32)

            def rope(c0, heads):
                v = z[:, :, c0:c0 + heads * HD].rearrange("p t (h w d) -> p t h w d", h=heads, w=2)
                x1, x2 = v[:, :, :, 0, :], v[:, :, :, 1, :]
                t = [prod[:, j, 0:TILES * heads * 32].rearrange("p (t h d) -> p t h d", t=TILES, h=heads) for j in range(4)]
                cb, sb_ = (m[:].unsqueeze(2).broadcast_to([P, TILES, heads, HD // 2]) for m in (cos, sin))
                dve.tensor_tensor(t[0], x1, cb, ALU.mult)
                dve.tensor_tensor(t[1], x2, sb_, ALU.mult)
                dve.tensor_tensor(t[2], x2, cb, ALU.mult)
                link(dve.tensor_tensor(t[3], x1, sb_, ALU.mult))
                link(dve.tensor_tensor(x1, t[0], t[1], ALU.subtract))
                dve.tensor_tensor(x2, t[2], t[3], ALU.add).then_inc(E["roped"], 1)
                return
            for n, (c0, heads) in enumerate(((0, NH), (C_K, NKV), (C_K + 2 * KVW, NKV), (C_K + 4 * KVW, NKV))):
                rope(c0, heads)
                dve.wait_ge(E["roped"], n + 1)

            link = own(dve, E["small_kept"])
            dve.wait_ge(E["csc_done"], NQ)
            dve.wait_ge(E["masks"], 6)
            sv = sc[:, :, 0:NH * NC_P].rearrange("p q (h c) -> p q h c", h=NH)
            over_h = lambda m: m[:].unsqueeze(2).broadcast_to([P, NQ, NH, NC_P])
            over_c = lambda m: m[:].unsqueeze(3).broadcast_to([P, NQ, NH, NC_P])
            link(dve.tensor_tensor(pc[:], sv, over_h(cneg), ALU.add))
            link(dve.tensor_reduce(cmx[:], pc[:], AX_X, ALU.max))
            dve.tensor_tensor(pc[:], pc[:], over_c(cmx), ALU.subtract).then_inc(E["cmx_ready"], 1)
            dve.wait_ge(E["cexp_ready"], 1)
            link(dve.tensor_tensor(pc[:], pc[:], over_h(c01), ALU.mult))
            link(dve.tensor_reduce(csum[:], pc[:], AX_X, ALU.add))
            link(dve.tensor_scalar(csum[:], csum[:], TINY, None, ALU.max))
            link(dve.reciprocal(csum[:], csum[:]))
            dve.wait_ge(E["gates_ready"], NKV)
            gv = gates[:, 0:NQ, :].rearrange("p t (h j) -> p t h j", j=3)
            dve.tensor_tensor(csum[:], csum[:], gv[:, :, :, 0], ALU.mult).then_inc(E["coefc_ready"], 1)
            dve.wait_ge(E["coefc_ready"], 1)
            for i in range(NQ):
                dve.wait_ge(E["cpv_done"], i + 1)
                dve.tensor_tensor(o[:, i, :].rearrange("p (g r d) -> p r g d", g=NKV, r=REP),
                                  oo[:, i % 2, :].rearrange("p (r g d) -> p r g d", g=NKV, r=REP),
                                  csum[:, i, :].rearrange("p (r g) -> p r g", g=NKV).unsqueeze(3)
                                  .broadcast_to([P, REP, NKV, HD]), ALU.mult).then_inc(E["ocmp_ready"], 1)
            dve.wait_ge(E["ocmp_ready"], NQ)

            def maxima(u):
                i, h = UNITS[u]
                b = u % 2
                dve.wait_ge(E["s_done"], u + 1)
                diag = sc[:, 2 * b:2 * b + 2, P * i:P * i + P]
                link(dve.tensor_tensor(diag, diag, causal[:].unsqueeze(1).broadcast_to([P, 2, P]), ALU.add))
                link(dve.tensor_reduce(nmax[:, b, :], sc[:, 2 * b:2 * b + 2, 0:P * i + P], AX_X, ALU.max))
                dve.tensor_scalar(nmax[:, b, :], nmax[:, b, :], -1.0, None, ALU.mult).then_inc(E["max_ready"], 1)

            maxima(0)
            for u, (i, h) in enumerate(UNITS):
                b = u % 2
                if u + 1 < len(UNITS):
                    maxima(u + 1)
                dve.wait_ge(E["t_done"], u + 1)
                if u >= 2:
                    dve.wait_ge(E["pv_done"], u - 1)
                dve.tensor_copy(probT[:, b, 1, 0:P * i + P], tp[:, 1, 0:P * i + P]).then_inc(E["pt1"], 1)
                dve.wait_ge(E["p_ready"], 2 * u + 2)
                link(dve.reciprocal(coef[:, b, :], psum_row[:, b, :]))
                link(dve.tensor_tensor(coef[:, b, :], coef[:, b, :], gates[:, i, gate(h) + 1:gate(h) + 3], ALU.mult))
                dve.wait_ge(E["pv_done"], u + 1)
                oh = o[:, i, HD * h:HD * h + HD]
                p0 = head(h)[0]
                link(dve.scalar_tensor_tensor(out=oh, in0=oo[:, b, p0:p0 + HD], scalar=coef[:, b, 0:1], in1=oh,
                                              op0=ALU.mult, op1=ALU.add))
                dve.scalar_tensor_tensor(out=oh, in0=oo[:, b, KVW + p0:KVW + p0 + HD], scalar=coef[:, b, 1:2], in1=oh,
                                         op0=ALU.mult, op1=ALU.add).then_inc(E["o_done"], 1)

        @block.scalar
        def _(act):
            for g in range(NKV):
                c = C_GATE + 3 * REP * g
                act.activation(gates[:].rearrange("p t (r g j) -> p t r g j", g=NKV, j=3)[:, :, :, g, :],
                               z[:, :, c:c + 3 * REP].rearrange("p t (r j) -> p t r j", j=3),
                               ACT.Sigmoid).then_inc(E["gates_ready"], 1)
            act.activation(S.gates_s[:], z[0:NB, 4, C_GATE:C_GATE + 3 * NH], ACT.Sigmoid).then_inc(E["gates_ready"], 1)
            for t in range(TILES):
                act.wait_ge(E["tr_done"], 2 * t + 1)
                act.activation(qT[:, :, P * t:P * t + P], tp[:, 0, :].rearrange("p (r n) -> p r n", r=REP), ACT.Copy,
                               scale=SCALE).then_inc(E["tr_kept"], 1)
                act.wait_ge(E["tr_done"], 2 * t + 2)
                j = 0 if t < NQ else 2
                act.activation(xT[:, j:4, P * t:P * t + P], tp[:, 1, :].rearrange("p (r n) -> p r n", r=4)[:, j:4],
                               ACT.Copy).then_inc(E["tr_kept"], 1)
            act.wait_ge(E["tr_kept"], 2 * TILES)
            act.activation(S.qTs[:], qT[:, :, SEQ:TOK], ACT.Copy)
            act.activation(S.kTs[:], xT[:, 2:4, SEQ:TOK], ACT.Copy)
            act.activation(S.vs[:], z[0:NB, 4, C_K + 3 * KVW:C_K + 4 * KVW], ACT.Copy)
            act.activation(S.vw[:], z[0:NB, 4, C_K + 5 * KVW:C_K + 6 * KVW], ACT.Copy)
            for j in range(2):
                act.wait_ge(E["hid_done"], j + 1)
                act.activation(hid[:, j, :], oo[0:NC_P + 2, j, 0:P], ACT.Copy).then_inc(E["hid_kept"], 1)
            act.wait_ge(E["hidT_done"], 1)
            for j in range(2):
                act.activation(S.hbias[:, j:j + 1], tp[:, 0, 64 * j + NC_P + 1:64 * j + NC_P + 2],
                               ACT.Copy).then_inc(E["bias_kept"], 1)
            act.wait_ge(E["bias_kept"], 2)
            for j in range(2):
                act.activation(gh[:, j, :], tp[:, 0, 64 * j:64 * j + NC_P], ACT.Gelu_apprx_tanh,
                               bias=S.hbias[:, j:j + 1]).then_inc(E["gh_ready"], 1)
            act.wait_ge(E["cmp_done"], 1)
            act.wait_ge(E["ck_zero"], 1)
            for g in range(NKV):
                act.activation(ckT[HD * g:HD * g + HD, g, :], oo[HD * g:HD * g + HD, 0, 0:NC_P],
                               ACT.Copy).then_inc(E["cmp_kept"], 1)
            act.activation(cv[:], oo[0:NC_P, 0, 128:128 + KVW], ACT.Copy).then_inc(E["cmp_kept"], 1)
            act.wait_ge(E["cmx_ready"], 1)
            act.activation(pc[:], pc[:], ACT.Exp).then_inc(E["cexp_ready"], 1)
            for i in range(NQ):
                act.wait_ge(E["ct_done"], i + 1)
                if i >= 1:
                    act.wait_ge(E["cpv_done"], i)
                act.activation(pcT[:], tp[0:NC_P, :, :].rearrange("p a b -> p (a b)"), ACT.Copy).then_inc(E["ct_kept"], 1)
            for u, (i, h) in enumerate(UNITS):
                b = u % 2
                act.wait_ge(E["max_ready"], u + 1)
                if u >= 2:
                    act.wait_ge(E["t_done"], u - 1)
                    act.wait_ge(E["o_done"], u - 1)
                for j in range(2):
                    act.activation(prob[:, b, j, 0:P * i + P], sc[:, 2 * b + j, 0:P * i + P], ACT.Exp,
                                   bias=nmax[:, b, j:j + 1], accum_out=psum_row[:, b, j:j + 1]).then_inc(E["p_ready"], 1)
                act.wait_ge(E["t_done"], u + 1)
                if u >= 2:
                    act.wait_ge(E["pv_done"], u - 1)
                act.activation(probT[:, b, 0, 0:P * i + P], tp[:, 0, 0:P * i + P], ACT.Copy).then_inc(E["pt0"], 1)
            for t in range(NQ):
                act.wait_ge(E["ot_done"], t + 1)
                act.activation(S.oT[:, :, P * t:P * t + P], sc[:, t, :].rearrange("p (k n) -> p k n", k=4),
                               ACT.Copy).then_inc(E["ot_kept"], 1)

        @block.tensor
        def _(pe):
            ident = S.ident
            pe.wait_ge(E["roped"], 4)
            for t in range(TILES):
                if t:
                    pe.wait_ge(E["tr_kept"], 2 * t - 1)
                for r in range(REP):
                    last = pe.transpose(tp[:, 0, P * r:P * r + P], z[:, t, P * r:P * r + P], ident[:])
                last.then_inc(E["tr_done"], 1)
                if t:
                    pe.wait_ge(E["tr_kept"], 2 * t)
                for j, k in enumerate((0, 1, 2, 4)):
                    c = C_K + KVW * k
                    last = pe.transpose(tp[:, 1, P * j:P * j + P], z[:, t, c:c + KVW], ident[:])
                last.then_inc(E["tr_done"], 1)
            pe.wait_ge(E["tr_kept"], 2 * TILES)
            pe.wait_ge(E["w_cmp"], 16 * 12)
            for j, w in enumerate((S.w1k, S.w1v)):
                for t in range(CMP_LEN):
                    last = pe.matmul(oo[0:NC_P + 2, j, 0:P], xT[:, j, t:t + CMP_STRIDE * (NC_P + 1) + 1:CMP_STRIDE],
                                     w[:, t, :], start=(t == 0), stop=(t == CMP_LEN - 1))
                last.then_inc(E["hid_done"], 1)
            pe.wait_ge(E["hid_kept"], 2)
            for j in range(2):
                last = pe.transpose(tp[:, 0, 64 * j:64 * j + NC_P + 2], hid[:, j, :], ident[0:NC_P + 2, 0:NC_P + 2])
            last.then_inc(E["hidT_done"], 1)
            pe.wait_ge(E["gh_ready"], 2)
            pe.matmul(oo[:, 0, 0:NC_P], S.w2k[:], gh[:, 0, :], start=True, stop=True)
            pe.matmul(oo[0:NC_P, 0, 128:128 + KVW], gh[:, 1, :], S.w2v[:], start=True, stop=True).then_inc(E["cmp_done"], 1)
            pe.wait_ge(E["cmp_kept"], 3)
            for i in range(NQ):
                for r in range(REP):
                    w = NKV * NC_P
                    last = pe.matmul(sc[:, i, w * r:w * r + w], qT[:, r, P * i:P * i + P],
                                     ckT[:].rearrange("p g c -> p (g c)"), start=True, stop=True)
                last.then_inc(E["csc_done"], 1)
            pe.wait_ge(E["coefc_ready"], 1)
            for i in range(NQ):
                if i:
                    pe.wait_ge(E["ct_kept"], i)
                for h in range(NH):
                    last = pe.transpose(tp[0:NC_P, h // 4, P * (h % 4):P * (h % 4) + P], pc[:, i, h, :], ident[:])
                last.then_inc(E["ct_done"], 1)
                pe.wait_ge(E["ct_kept"], i + 1)
                if i >= 2:
                    pe.wait_ge(E["ocmp_ready"], i - 1)
                for h in range(NH):
                    p0 = HD * (h % NKV)
                    last = pe.matmul(oo[:, i % 2, HD * h:HD * h + HD], pcT[:, P * h:P * h + P], cv[:, p0:p0 + HD],
                                     start=True, stop=True)
                last.then_inc(E["cpv_done"], 1)
            pe.wait_ge(E["ocmp_ready"], NQ)

            def scores(u):
                i, h = UNITS[u]
                b = u % 2
                p0, r = head(h)
                if u >= 2:
                    pe.wait_ge(E["p_ready"], 2 * u - 2)
                for j in range(2):
                    last = pe.matmul(sc[:, 2 * b + j, 0:P * i + P], qT[p0:p0 + HD, r, P * i:P * i + P],
                                     xT[p0:p0 + HD, 2 + j, 0:P * i + P], start=True, stop=True)
                last.then_inc(E["s_done"], 1)

            scores(0)
            for u, (i, h) in enumerate(UNITS):
                b = u % 2
                p0, r = head(h)
                if u + 1 < len(UNITS):
                    scores(u + 1)
                pe.wait_ge(E["p_ready"], 2 * u + 2)
                if u:
                    pe.wait_ge(E["pt0"], u)
                    pe.wait_ge(E["pt1"], u)
                for j in range(2):
                    for k in range(i + 1):
                        last = pe.transpose(tp[:, j, P * k:P * k + P], prob[:, b, j, P * k:P * k + P], ident[:])
                last.then_inc(E["t_done"], 1)
                pe.wait_ge(E["pt0"], u + 1)
                pe.wait_ge(E["pt1"], u + 1)
                if u >= 2:
                    pe.wait_ge(E["o_done"], u - 1)
                for j, c in enumerate((C_K + 3 * KVW, C_K + 5 * KVW)):
                    for k in range(i + 1):
                        last = pe.matmul(oo[:, b, KVW * j:KVW * j + KVW], probT[:, b, j, P * k:P * k + P],
                                         z[:, k, c:c + KVW], start=(k == 0), stop=(k == i))
                last.then_inc(E["pv_done"], 1)
            pe.wait_ge(E["o_done"], len(UNITS))
            for t in range(NQ):
                for k in range(4):
                    last = pe.transpose(sc[:, t, P * k:P * k + P], o[:, t, P * k:P * k + P], ident[:])
                last.then_inc(E["ot_done"], 1)


def stage_decode(nc, io, S):
    ROWS = NB * NH
    WB = io["cache_k_win"].shape[2]
    WT = WB // P
    DIAG = 72
    NSEL = PAST + 1
    with ExitStack() as ctx:
        sb = lambda n, s, d=F32: ctx.enter_context(nc.sbuf_tensor("de_" + n, s, d))
        sems = []
        sem = lambda n: new_semaphore(nc, ctx, sems, n)
        pages = sb("pages", [1, NB * NPG], I32)
        ptab = sb("ptab", [P, NB * NPG], I32)
        tok = sb("tok", [P, NB * NPG])
        row_of = sb("row_of", [P, NB * NPG], U32)
        nat = sb("nat", [P, 2, NPG + WT, KVW])
        xT = sb("xT", [P, NB, PAST])
        kT = sb("kT", [P, 2, PAST + WB])
        vsel = sb("vsel", [P, NB, NPG, KVW])
        vwin = sb("vwin", [P, NB, WT, KVW])
        qbd = sb("qbd", [P, NB * DIAG])
        qall = sb("qall", [P, ROWS])
        ghs = sb("ghs", [P, NB * NC_S])
        ckT = sb("ckT", [P, NB, NC_S])
        cv = sb("cv", [NC_S, NB, KVW])
        touch = sb("touch", [NC_S, NS_S])
        same = sb("same", [ROWS, ROWS])
        seq = sb("seq", [ROWS, NB])
        grp = sb("grp", [ROWS, NKV])
        grow = sb("grow", [ROWS, 3])
        pcs = sb("pcs", [ROWS, NC_S])
        pcT = sb("pcT", [NC_S, ROWS])
        pcm = sb("pcm", [NC_S, NB * DIAG])
        impr = sb("impr", [ROWS, NS_S])
        imp = sb("imp", [ROWS, NS_S])
        jdx = sb("jdx", [ROWS, 16])
        tie = sb("tie", [ROWS, 16])
        drop = sb("drop", [ROWS, 16])
        st = sb("st", [ROWS, 16])
        s_win = sb("s_win", [ROWS, WB + 1])
        junk = sb("junk_d", [ROWS, NB])
        anew = sb("anew", [ROWS, 2, NB])
        anT = sb("anT", [NB, 2, ROWS])
        wgt = sb("wgt", [ROWS, 3, NKV])
        od = sb("od", [ROWS, HD])
        flat = xT[:].rearrange("p b n -> p (b n)")
        psm = flat[:, 0:NPG * 8 * DIAG].rearrange("p (c n) -> p c n", c=NPG)
        pwm = flat[:, NPG * 8 * DIAG:(NPG + WT) * 8 * DIAG].rearrange("p (c n) -> p c n", c=WT)
        s_sel = flat[0:ROWS, (NPG + WT) * 8 * DIAG:(NPG + WT) * 8 * DIAG + NSEL]
        scratch = nc.dram_tensor("gate_rows", [NB, 3 * NH], F32).ap()
        ps = lambda n, s: ctx.enter_context(nc.psum_tensor(n, s, F32))
        tp = ps("dtp", [P, 2, 512])
        ph = ps("dph", [P, 512])
        po = ps("dpo", [P, 2, 512])
        ssel = ps("dssel", [ROWS, 2, 512])
        swin = ps("dswin", [ROWS, 512])
        names = ("consts", "table", "zeroed", "wlanded", "ptab", "rows_known", "nat_used", "tr_done", "kept0", "kept1", "hid_done", "gh_ready",
                 "w2_done", "cmp_kept", "q_ready", "sc_done", "c_max", "c_exp", "c_ready", "ct_done", "ct_kept",
                 "pcm_ready", "imp_done", "impr_kept", "imp2_done", "ds_done", "new_done", "sel_max", "sel_exp",
                 "win_max", "win_exp", "room", "pt_done", "pt_kept", "an_ready", "anT_done", "anT_kept", "oc_done",
                 "os_done", "ow_done", "od_ready", "odT_done", "odT_kept", "dve_own", "g_saved", "iota")
        E = {n: sem("de_" + n) for n in names}
        landed = [sem("nat_landed0"), sem("nat_landed1")]
        vlanded = S.gather_sem
        batches = [(a, b, f) for a in range(3) for b in range(NB) for f in range(0, NPG + (WT if a == 2 else 0), 4)]
        block = open_block(nc, ctx, sems)

        @block.gpsimd
        def _(pool):
            pool.sem_inc(E["nat_used"], 2)
            for m in (qbd, qall, pcm):
                pool.memset(m[:], 0.0).then_inc(E["zeroed"], 1)
            pool.iota(jdx[:], [[1, 16]], base=0, channel_multiplier=0,
                      allow_small_or_imprecise_dtypes=True).then_inc(E["iota"], 1)
            pool.iota(tok[:], [[0, NB * NPG]], base=0, channel_multiplier=1,
                      allow_small_or_imprecise_dtypes=True).then_inc(E["iota"], 1)
            pool.wait_ge(E["rows_known"], 1)
            src = io["cache_v_sel"].rearrange("a n t g d -> (a n t) (g d)")
            for b in range(NB):
                for k in range(NPG):
                    pool.indirect_dma_start(vsel[:, b, k, :], None, src, bass.IndirectOffsetOnAxis(
                        ap=row_of[:, NPG * b + k:NPG * b + k + 1], axis=0)).then_inc(vlanded, 16)
            pool.wait_ge(E["hid_done"], 2)
            pool.memset(flat[:, 0:(NPG + WT) * 8 * DIAG], 0.0).then_inc(E["room"], 1)

        @block.sync
        def _(sp):
            sp.dma_start(pages[:], io["page_table"].rearrange("b n -> (b n)").unsqueeze(0)).then_inc(E["table"], 16)
            sp.dma_start(ptab[:], io["page_table"].rearrange("b n -> (b n)").partition_broadcast(P)).then_inc(E["ptab"], 16)
            sp.dma_start(scratch, S.gates_s[:]).then_inc(E["g_saved"], 16)
            for m, name in ((touch, "c_touch"), (same, "c_same"), (seq, "c_seq"), (grp, "c_group")):
                sp.dma_start(m[:], io[name]).then_inc(E["consts"], 16)
            sp.wait_ge(E["table"], 16)
            sp.wait_ge(E["g_saved"], 16)
            sp.dma_start(grow[:], scratch.rearrange("b (h j) -> (b h) j", j=3)).then_inc(E["consts"], 16)
            for a, name in enumerate(("cache_k_cmp", "cache_v_cmp", "cache_k_sel")):
                src = io[name].rearrange("a n t g d -> (a n) t (g d)")
                with sp.Fori(0, NB // 2) as j:
                    for bb in range(2):
                        sp.wait_ge(E["nat_used"], 2 * j + (NB * a + bb + 1))
                        for k in range(NPG):
                            page = sp.value_load(pages[0:1, bass.ds(2 * NPG * j + (NPG * bb + k), 1)], min_val=0,
                                                 max_val=io[name].shape[1] - 1)
                            sp.dma_start(nat[:, bb, k, :], src[bass.ds(page, 1)].rearrange("a t n -> (a t) n"))\
                              .then_inc(landed[bb], 16)
                        if a == 2:
                            win = io["cache_k_win"].rearrange("a b (w p) g d -> p (a b) w (g d)", p=P)
                            sp.dma_start(nat[:, bb, NPG:NPG + WT, :], win[:, bass.ds(2 * j + bb, 1)]
                                         .rearrange("p b w n -> p (b w) n")).then_inc(landed[bb], 16)
                if a == 0:
                    for b in range(NB):
                        sp.dma_start(vwin[:, b], io["cache_v_win"]
                                     .rearrange("a b (w p) g d -> p (a b) w (g d)", p=P)[:, b]).then_inc(E["wlanded"], 16)

        def evacuate(eng, copy, mine, done, kept, a_pass):
            for n, (a, b, f) in enumerate(batches):
                if a != a_pass or n % 2 != mine:
                    continue
                eng.wait_ge(done, n + 1)
                if a == 1:
                    eng.wait_ge(E["hid_done"], 1)
                if a == 2 and b >= 2:
                    eng.wait_ge(E["ds_done"], b - 1)
                to = xT[:, b, P * f:P * f + 512] if a < 2 else kT[:, b % 2, P * f:P * f + 512]
                copy(to, tp[:, n % 2, :]).then_inc(kept, 1)

        @block.scalar
        def _(act):
            copy = lambda to, of: act.activation(to, of, ACT.Copy)
            for a in range(3):
                evacuate(act, copy, 0, E["tr_done"], E["kept0"], a)
                if a < 2:
                    act.wait_ge(E["hid_done"], a + 1)
                    if a:
                        act.wait_ge(E["w2_done"], 1)
                    act.activation(ghs[:], ph[:, 0:NB * NC_S], ACT.Gelu_apprx_tanh,
                                   bias=S.hbias[:, a:a + 1]).then_inc(E["gh_ready"], 1)
                    act.wait_ge(E["w2_done"], a + 1)
                    if a == 0:
                        copy(ckT[:].rearrange("p b c -> p (b c)"), po[:, 0, 0:NB * NC_S]).then_inc(E["cmp_kept"], 1)
                    else:
                        copy(cv[:].rearrange("c b n -> c (b n)"),
                             po[0:NC_S, :, :].rearrange("c a n -> c (a n)")).then_inc(E["cmp_kept"], 1)
            act.wait_ge(E["c_max"], 1)
            act.activation(pcs[:], ph[0:ROWS, 0:NC_S], ACT.Exp, bias=st[:, 0:1], accum_out=st[:, 1:2]).then_inc(E["c_exp"], 1)
            act.wait_ge(E["ct_done"], 1)
            copy(pcT[:], tp[0:NC_S, 0, 0:ROWS]).then_inc(E["ct_kept"], 1)
            act.wait_ge(E["imp_done"], 1)
            copy(impr[:], tp[0:ROWS, 1, 0:NS_S]).then_inc(E["impr_kept"], 1)
            act.wait_ge(E["sel_max"], 1)
            act.activation(s_sel, s_sel, ACT.Exp, bias=st[:, 2:3], accum_out=st[:, 3:4]).then_inc(E["sel_exp"], 1)
            act.wait_ge(E["win_max"], 1)
            act.activation(s_win[:], s_win[:], ACT.Exp, bias=st[:, 4:5], accum_out=st[:, 5:6]).then_inc(E["win_exp"], 1)
            act.wait_ge(E["anT_done"], 1)
            copy(anT[:].rearrange("b j n -> b (j n)"), ph[0:NB, 0:2 * ROWS]).then_inc(E["anT_kept"], 1)
            act.wait_ge(E["odT_done"], 1)
            for w in range(2):
                copy(S.oT[HD * w:HD * w + HD, :, SEQ:TOK],
                     tp[0:HD, 0, 0:ROWS].rearrange("d (b j w) -> d w j b", j=4, w=2)[:, w]).then_inc(E["odT_kept"], 1)

        @block.vector
        def _(dve):
            link = own(dve, E["dve_own"])
            copy = lambda to, of: dve.tensor_copy(to, of)
            dve.wait_ge(E["ptab"], 16)
            dve.wait_ge(E["iota"], 2)
            dve.scalar_tensor_tensor(out=row_of[:], in0=ptab[:], scalar=float(PAGE), in1=tok[:], op0=ALU.mult,
                                     op1=ALU.add).then_inc(E["rows_known"], 1)
            dve.wait_ge(E["zeroed"], 3)
            for g in range(NKV):
                p = slice(HD * g, HD * g + HD)
                q = S.qTs[p].rearrange("p r b -> p b r")
                copy(qbd[p].rearrange("p (b n) -> p b n", n=DIAG)[:, :, REP * g:REP * g + REP], q).then_inc(E["q_ready"], 1)
                copy(qall[p].rearrange("p (b n) -> p b n", n=NH)[:, :, REP * g:REP * g + REP], q).then_inc(E["q_ready"], 1)
            for a in range(3):
                evacuate(dve, copy, 1, E["tr_done"], E["kept1"], a)
            dve.wait_ge(E["sc_done"], 1)
            link(dve.tensor_reduce(st[:, 0:1], ph[0:ROWS, 0:NC_S], AX_X, ALU.max))
            dve.tensor_scalar(st[:, 0:1], st[:, 0:1], -1.0, None, ALU.mult).then_inc(E["c_max"], 1)
            dve.wait_ge(E["c_exp"], 1)
            link(dve.tensor_scalar(st[:, 1:2], st[:, 1:2], TINY, None, ALU.max))
            link(dve.reciprocal(st[:, 1:2], st[:, 1:2]))
            dve.tensor_scalar(pcs[:], pcs[:], st[:, 1:2], None, ALU.mult).then_inc(E["c_ready"], 1)
            dve.wait_ge(E["ct_kept"], 1)
            copy(pcm[:].rearrange("c (b n) -> c b n", n=DIAG)[:, :, 0:NH],
                 pcT[:].rearrange("c (b n) -> c b n", n=NH)).then_inc(E["pcm_ready"], 1)
            dve.wait_ge(E["imp2_done"], 1)
            free = slice(1, NS_S - 2)
            nf = NS_S - 3
            link(copy(imp[:], tp[0:ROWS, 0, 0:NS_S]))
            link(dve.tensor_reduce(st[:, 6:7], imp[:, free], AX_X, ALU.min))
            link(dve.tensor_scalar(tie[:, 0:nf], imp[:, free], st[:, 6:7], None, ALU.is_equal))
            dve.wait_ge(E["iota"], 1)
            link(dve.tensor_tensor(tie[:, 0:nf], tie[:, 0:nf], jdx[:, free], ALU.mult))
            link(dve.tensor_reduce(st[:, 7:8], tie[:, 0:nf], AX_X, ALU.max))
            link(dve.tensor_scalar(drop[:], jdx[:], st[:, 7:8], NEG, ALU.is_equal, ALU.mult))
            dve.wait_ge(E["ds_done"], NB)
            dve.wait_ge(E["new_done"], 1)
            link(dve.tensor_tensor(s_sel[:, 0:PAST].rearrange("p (j n) -> p j n", n=SEL_BLOCK),
                                   ssel[:].rearrange("p a n -> p (a n)").rearrange("p (j n) -> p j n", n=SEL_BLOCK),
                                   drop[:].unsqueeze(2).broadcast_to([ROWS, 16, SEL_BLOCK]), ALU.add))
            for j, to in enumerate((s_sel[:, PAST:PAST + 1], s_win[:, WB:WB + 1])):
                link(dve.scalar_tensor_tensor(out=junk[:], in0=po[0:ROWS, 0, NB * j:NB * j + NB], scalar=1.0, in1=seq[:],
                                              op0=ALU.mult, op1=ALU.mult, accum_out=to))
            link(dve.tensor_reduce(st[:, 2:3], s_sel, AX_X, ALU.max))
            dve.tensor_scalar(st[:, 2:3], st[:, 2:3], -1.0, None, ALU.mult).then_inc(E["sel_max"], 1)
            link(copy(s_win[:, 0:WB], swin[:]))
            link(dve.memset(s_win[:, 0:1], NEG))
            link(dve.tensor_reduce(st[:, 4:5], s_win[:], AX_X, ALU.max))
            dve.tensor_scalar(st[:, 4:5], st[:, 4:5], -1.0, None, ALU.mult).then_inc(E["win_max"], 1)
            for j, (done, p) in enumerate((("sel_exp", s_sel[:, PAST:PAST + 1]), ("win_exp", s_win[:, WB:WB + 1]))):
                dve.wait_ge(E[done], 1)
                dve.tensor_scalar(anew[:, j, :], seq[:], p, None, ALU.mult).then_inc(E["an_ready"], 1)
            dve.wait_ge(E["room"], 1)
            for n, (to, chunks) in enumerate(((psm, NPG), (pwm, WT))):
                dve.wait_ge(E["pt_done"], n + 1)
                copy_to = to.rearrange("p c (b n) -> p c b n", n=DIAG)[:, :, :, 0:NH]
                copy(copy_to, tp[:, n, 0:chunks * ROWS].rearrange("p (c b n) -> p c b n", c=chunks, b=NB))\
                    .then_inc(E["pt_kept"], 1)
            dve.wait_ge(E["consts"], 16 * 5)
            link(dve.tensor_scalar(st[:, 3:4], st[:, 3:4], TINY, None, ALU.max))
            link(dve.tensor_scalar(st[:, 5:6], st[:, 5:6], TINY, None, ALU.max))
            link(dve.reciprocal(st[:, 3:4], st[:, 3:4]))
            link(dve.reciprocal(st[:, 5:6], st[:, 5:6]))
            link(dve.tensor_scalar(wgt[:, 0, :], grp[:], grow[:, 0:1], None, ALU.mult))
            link(dve.tensor_scalar(wgt[:, 1, :], grp[:], grow[:, 1:2], st[:, 3:4], ALU.mult, ALU.mult))
            link(dve.tensor_scalar(wgt[:, 2, :], grp[:], grow[:, 2:3], st[:, 5:6], ALU.mult, ALU.mult))
            for j, (done, bank) in enumerate((("oc_done", po[0:ROWS, 1, 0:KVW]), ("os_done", ph[0:ROWS, 128:128 + KVW]),
                                              ("ow_done", swin[:, 0:KVW]))):
                dve.wait_ge(E[done], 1)
                for g in range(NKV):
                    half = bank[:, HD * g:HD * g + HD]
                    if j == 0 and g == 0:
                        link(dve.tensor_scalar(od[:], half, wgt[:, 0, 0:1], None, ALU.mult))
                    else:
                        ins = dve.scalar_tensor_tensor(out=od[:], in0=half, scalar=wgt[:, j, g:g + 1], in1=od[:],
                                                       op0=ALU.mult, op1=ALU.add)
                        if j == 2 and g == 1:
                            ins.then_inc(E["od_ready"], 1)
                        else:
                            link(ins)

        @block.tensor
        def _(pe):
            use = {0: 0, 1: 0}
            count = {0: 0, 1: 0}
            pe.wait_ge(E["q_ready"], 2 * NKV)
            for n, (a, b, f) in enumerate(batches):
                last_of = f + 4 == NPG + (WT if a == 2 else 0)
                if f == 0:
                    count[b % 2] += 16 * (NPG + (1 if a == 2 else 0))
                    pe.wait_ge(landed[b % 2], count[b % 2])
                if n >= 2:
                    pe.wait_ge(E["kept%d" % (n % 2)], n // 2)
                for k in range(4):
                    last = pe.transpose(tp[:, n % 2, P * k:P * k + P], nat[:, b % 2, f + k, :], S.ident[:])
                last.then_inc(E["tr_done"], 1)
                if last_of:
                    pe.wait_ge(E["tr_done"], n + 1)
                    pe.sem_inc(E["nat_used"], 1)
                if a == 2 and last_of:
                    pe.wait_ge(E["kept0"], (n + 2) // 2)
                    pe.wait_ge(E["kept1"], (n + 1) // 2)
                    for j in range(2):
                        pe.matmul(ssel[:, j, :], qbd[:, ROWS * b:ROWS * b + ROWS], kT[:, b % 2, 512 * j:512 * j + 512],
                                  start=(b == 0), stop=(b == NB - 1))
                    pe.matmul(swin[:], qbd[:, ROWS * b:ROWS * b + ROWS], kT[:, b % 2, PAST:PAST + WB],
                              start=(b == 0), stop=(b == NB - 1)).then_inc(E["ds_done"], 1)
                if a < 2 and last_of and b == NB - 1:
                    pe.wait_ge(E["kept0"], (n + 2) // 2)
                    pe.wait_ge(E["kept1"], (n + 1) // 2)
                    if a:
                        pe.wait_ge(E["cmp_kept"], 1)
                    w = (S.w1k, S.w1v)[a]
                    for s in range(CMP_LEN):
                        last = pe.matmul(ph[:, 0:NB * NC_S], w[:, s, :],
                                         xT[:, :, s:s + CMP_STRIDE * (NC_S - 1) + 1:CMP_STRIDE],
                                         start=(s == 0), stop=(s == CMP_LEN - 1))
                    last.then_inc(E["hid_done"], 1)
                    pe.wait_ge(E["gh_ready"], a + 1)
                    if a == 0:
                        pe.matmul(po[:, 0, 0:NB * NC_S], S.w2k[:], ghs[:], start=True, stop=True).then_inc(E["w2_done"], 1)
                    else:
                        for c in range(NB):
                            last = pe.matmul(po[0:NC_S, c // 4, KVW * (c % 4):KVW * (c % 4) + KVW],
                                             ghs[:, NC_S * c:NC_S * c + NC_S], S.w2v[:], start=True, stop=True)
                        last.then_inc(E["w2_done"], 1)
            N = len(batches)
            pe.wait_ge(E["cmp_kept"], 2)
            for b in range(NB):
                last = pe.matmul(ph[0:ROWS, 0:NC_S], qbd[:, ROWS * b:ROWS * b + ROWS], ckT[:, b, :],
                                 start=(b == 0), stop=(b == NB - 1))
            last.then_inc(E["sc_done"], 1)
            for j in range(2):
                last = pe.matmul(po[0:ROWS, 0, NB * j:NB * j + NB], qall[:], S.kTs[:, j, :], start=True, stop=True)
            last.then_inc(E["new_done"], 1)
            pe.wait_ge(E["kept0"], N // 2)
            pe.wait_ge(E["kept1"], N // 2)
            pe.wait_ge(E["c_ready"], 1)
            pe.transpose(tp[0:NC_S, 0, 0:ROWS], pcs[:], S.ident[0:ROWS, 0:ROWS]).then_inc(E["ct_done"], 1)
            pe.wait_ge(E["ct_kept"], 1)
            pe.wait_ge(E["consts"], 16 * 5)
            pe.matmul(tp[0:ROWS, 1, 0:NS_S], pcT[:], touch[:], start=True, stop=True).then_inc(E["imp_done"], 1)
            pe.wait_ge(E["impr_kept"], 1)
            pe.matmul(tp[0:ROWS, 0, 0:NS_S], same[:], impr[:], start=True, stop=True).then_inc(E["imp2_done"], 1)
            pe.wait_ge(E["pcm_ready"], 1)
            for b in range(NB):
                last = pe.matmul(po[0:ROWS, 1, 0:KVW], pcm[:, ROWS * b:ROWS * b + ROWS], cv[:, b, :],
                                 start=(b == 0), stop=(b == NB - 1))
            last.then_inc(E["oc_done"], 1)
            pe.wait_ge(E["sel_exp"], 1)
            for c in range(NPG):
                last = pe.transpose(tp[:, 0, ROWS * c:ROWS * c + ROWS], s_sel[:, P * c:P * c + P], S.ident[0:ROWS, 0:ROWS])
            last.then_inc(E["pt_done"], 1)
            pe.wait_ge(E["win_exp"], 1)
            for c in range(WT):
                last = pe.transpose(tp[:, 1, ROWS * c:ROWS * c + ROWS], s_win[:, P * c:P * c + P], S.ident[0:ROWS, 0:ROWS])
            last.then_inc(E["pt_done"], 1)
            pe.wait_ge(E["an_ready"], 2)
            for j in range(2):
                last = pe.transpose(ph[0:NB, ROWS * j:ROWS * j + ROWS], anew[:, j, :], S.ident[0:ROWS, 0:ROWS])
            last.then_inc(E["anT_done"], 1)
            pe.wait_ge(E["anT_kept"], 1)
            pe.wait_ge(vlanded, 16 * NB * NPG)
            pe.wait_ge(E["wlanded"], 16 * NB)
            for n, (done, bank, probs, vals, new, chunks) in enumerate((
                    ("os_done", ph[0:ROWS, 128:128 + KVW], psm, vsel, S.vs, NPG),
                    ("ow_done", swin[:, 0:KVW], pwm, vwin, S.vw, WT))):
                pe.wait_ge(E["pt_kept"], n + 1)
                for b in range(NB):
                    for c in range(chunks):
                        pe.matmul(bank, probs[:, c, ROWS * b:ROWS * b + ROWS], vals[:, b, c, :],
                                  start=(b == 0 and c == 0), stop=False)
                pe.matmul(bank, anT[:, n, :], new[:], start=False, stop=True).then_inc(E[done], 1)
            pe.wait_ge(E["od_ready"], 1)
            pe.transpose(tp[0:HD, 0, 0:ROWS], od[:], S.ident[0:ROWS, 0:ROWS]).then_inc(E["odT_done"], 1)


def stage_state_space(nc, io, S):
    TWO_PI = 2 * math.pi
    C1 = 6.28125
    C2 = float(np.float32(np.round((TWO_PI - C1) * 2 ** 21) / 2 ** 21))
    C3 = float(np.float32(TWO_PI - C1 - C2))
    STEPS = SEQ.bit_length() - 1
    STEP = 160
    with ExitStack() as ctx:
        sb = lambda n, s, d=F32: ctx.enter_context(nc.sbuf_tensor("ss_" + n, s, d))
        sems = []
        sem = lambda n: new_semaphore(nc, ctx, sems, "ss_" + n)
        col = lambda n: sb(n, [P, NT_ST])
        a_re, a_im, ldt, mag, th = col("a_re"), col("a_im"), col("ldt"), col("mag"), col("th")
        s2, s4, c2, cm1, sn = col("s2"), col("s4"), col("c2"), col("cm1"), col("sn")
        ab_re, ab_im, nr, t0, t1, f_re, f_im = (col(n) for n in ("ab_re", "ab_im", "nr", "t0", "t1", "f_re", "f_im"))
        turns = sb("turns", [P, NT_ST], I32)
        b_in = sb("b_in", [P, 2, NT_ST, GRP_CH])
        c_in = sb("c_in", [P, 2, NT_ST, GRP_CH])
        bt = sb("bt", [P, 2, NT_ST, GRP_CH])
        skip = sb("skip", [P, 4])
        h0 = sb("h0", [P, 2, NT_ST, NB])
        hn = sb("hn", [P, 2, NT_ST, NB])
        ht = sb("ht", [P, 2, NT_ST, NB])
        last_h = sb("last_h", [P, 2, NT_ST])
        pw = sb("pw", [P, 2, STEPS, NT_ST])
        b_pad = sb("b_pad", [P, 2, 4, 4 * STEP])
        c_pad = sb("c_pad", [P, 3, 4, 4 * STEP])
        bT = sb("bT", [P, 2, NT_ST, P])
        tab = sb("tab", [P, 2, 2, 4, SEQ])
        q = sb("q", [P, 4, 4, SEQ // 2])
        m = sb("m", [P, 4, SEQ])
        w = sb("w", [P, 2, SEQ])
        g = sb("g", [P, 2, SEQ])
        zb = sb("zb", [P, 2, 4, SEQ])
        y = sb("y", [P, 2, 4 * NB])
        bu = ctx.enter_context(nc.psum_tensor("ss_bu", [P, 2, 2, SEQ], F32))
        yp = ctx.enter_context(nc.psum_tensor("ss_yp", [P, 2, SEQ], F32))
        bus = ctx.enter_context(nc.psum_tensor("ss_bus", [P, SEQ], F32))
        yps = ctx.enter_context(nc.psum_tensor("ss_yps", [P, SEQ], F32))
        names = ("landed", "zeroed", "a_scaled", "exps", "halved", "sines", "own", "pool_own", "padded", "b_done", "b_kept",
                 "table_ready", "bu_ready", "rot_done", "z_ready", "y_done", "bus_ready", "hn_ready", "ys_done",
                 "y_ready", "gelu_done", "stored", "powers", "ysum", "hs_kept")
        E = {n: sem(n) for n in names}
        block = open_block(nc, ctx, sems)
        LOADS = 11

        @block.sync
        def _(sp):
            for to, name in ((a_re, "a_re"), (a_im, "a_im"), (skip, "d_skip")):
                sp.dma_start(to[:], io[name]).then_inc(E["landed"], 16)
            for r in range(2):
                sp.dma_start(ldt[STATE * r:STATE * r + STATE, :],
                             io["log_dt"][r].partition_broadcast(STATE))\
                  .then_inc(E["landed"], 16)
            for j, part in enumerate(("re", "im")):
                sp.dma_start(b_in[:, j], io["b_" + part]).then_inc(E["landed"], 16)
                sp.dma_start(c_in[:, j], io["c_" + part]).then_inc(E["landed"], 16)
                sp.dma_start(h0[:, j], io["h0_" + part]).then_inc(E["landed"], 16)
            sp.wait_ge(E["z_ready"], NT_ST)
            sp.wait_ge(E["ysum"], NT_ST)
            sp.dma_start(io["p_ssm"], last_h[:]).then_inc(E["stored"], 16)
            sp.wait_ge(E["hn_ready"], 1)
            sp.dma_start(io["s_ssm"], hn[:]).then_inc(E["stored"], 16)
            sp.wait_ge(E["stored"], 32)

        @block.gpsimd
        def _(pool):
            pool.memset(b_pad[:], 0.0).then_inc(E["zeroed"], 1)
            pool.memset(c_pad[:], 0.0).then_inc(E["zeroed"], 1)
            link = own(pool, E["pool_own"])
            pool.wait_ge(E["powers"], 1)
            for u in range(4):
                b = u % 2
                if u >= 2:
                    pool.wait_ge(E["z_ready"], 4 * (u - 1))
                co, si = tab[:, b, 0], tab[:, b, 1]
                pool.memset(co[:, :, 0:1], 1.0)
                link(pool.memset(si[:, :, 0:1], 0.0))
                for k in range(STEPS):
                    n = 1 << k
                    pr, pi = (pw[:, j, k, 4 * u:4 * u + 4].unsqueeze(2).broadcast_to([P, 4, n]) for j in range(2))
                    pool.tensor_tensor(q[:, 0, :, 0:n], co[:, :, 0:n], pr, ALU.mult)
                    pool.tensor_tensor(q[:, 1, :, 0:n], si[:, :, 0:n], pi, ALU.mult)
                    pool.tensor_tensor(q[:, 2, :, 0:n], si[:, :, 0:n], pr, ALU.mult)
                    link(pool.tensor_tensor(q[:, 3, :, 0:n], co[:, :, 0:n], pi, ALU.mult))
                    pool.tensor_tensor(co[:, :, n:2 * n], q[:, 0, :, 0:n], q[:, 1, :, 0:n], ALU.subtract)
                    ins = pool.tensor_tensor(si[:, :, n:2 * n], q[:, 2, :, 0:n], q[:, 3, :, 0:n], ALU.add)
                    if k == STEPS - 1:
                        ins.then_inc(E["table_ready"], 1)
                        pool.wait_ge(E["table_ready"], u + 1)
                    else:
                        link(ins)

        @block.scalar
        def _(act):
            act.wait_ge(E["landed"], 16 * LOADS)
            act.activation(ldt[:], ldt[:], ACT.Exp).then_inc(E["exps"], 1)
            act.wait_ge(E["a_scaled"], 1)
            act.activation(mag[:], mag[:], ACT.Exp).then_inc(E["exps"], 1)
            act.wait_ge(E["halved"], 1)
            act.activation(s2[:], th[:], ACT.Sin, scale=0.5).then_inc(E["sines"], 1)
            act.activation(s4[:], th[:], ACT.Sin, scale=0.25).then_inc(E["sines"], 1)
            for n in range(8):
                act.wait_ge(E["b_done"], n + 1)
                act.activation(bT[:, n // 4, 4 * (n % 4):4 * (n % 4) + 4, :].rearrange("p t n -> p (t n)"),
                               bu[:, (n % 4) // 2, n % 2, :], ACT.Copy).then_inc(E["b_kept"], 1)
            for u in range(4):
                act.wait_ge(E["y_ready"], u + 1)
                act.activation(S.uT[:, u, 0:SEQ], S.uT[:, u, 0:SEQ], ACT.Gelu_apprx_tanh).then_inc(E["gelu_done"], 1)
            act.wait_ge(E["hs_kept"], 1)
            act.activation(S.uT[:, :, SEQ:TOK], y[:, 1, 0:4 * NB].rearrange("p (u b) -> p u b", b=NB),
                           ACT.Gelu_apprx_tanh).then_inc(E["gelu_done"], 1)

        @block.vector
        def _(dve):
            link = own(dve, E["own"])
            tt = lambda o_, x_, y_, op: dve.tensor_tensor(o_, x_, y_, op)
            dve.wait_ge(E["exps"], 1)
            link(tt(th[:], a_im[:], ldt[:], ALU.mult))
            tt(mag[:], a_re[:], ldt[:], ALU.mult).then_inc(E["a_scaled"], 1)
            link(dve.tensor_scalar(t0[:], th[:], 1.0 / TWO_PI, None, ALU.mult))
            link(dve.tensor_copy(turns[:], t0[:]))
            link(dve.tensor_copy(t0[:], turns[:]))
            for c in (C1, C2, C3):
                ins = dve.scalar_tensor_tensor(out=th[:], in0=t0[:], scalar=-c, in1=th[:], op0=ALU.mult, op1=ALU.add)
                if c is C3:
                    ins.then_inc(E["halved"], 1)
                else:
                    link(ins)
            link(tt(f_re[:], a_re[:], a_re[:], ALU.mult))
            link(tt(f_im[:], a_im[:], a_im[:], ALU.mult))
            link(tt(t1[:], f_re[:], f_im[:], ALU.add))
            link(dve.reciprocal(t1[:], t1[:]))
            dve.wait_ge(E["sines"], 2)
            link(tt(c2[:], s4[:], s4[:], ALU.mult))
            link(dve.tensor_scalar(c2[:], c2[:], -2.0, 1.0, ALU.mult, ALU.add))
            link(dve.scalar_tensor_tensor(out=sn[:], in0=s2[:], scalar=2.0, in1=c2[:], op0=ALU.mult, op1=ALU.mult))
            link(dve.scalar_tensor_tensor(out=cm1[:], in0=s2[:], scalar=-2.0, in1=s2[:], op0=ALU.mult, op1=ALU.mult))
            link(dve.tensor_scalar(pw[:, 0, 0, :], cm1[:], 1.0, None, ALU.add))
            link(dve.tensor_copy(pw[:, 1, 0, :], sn[:]))
            for k in range(1, STEPS):
                r, i = pw[:, 0, k - 1, :], pw[:, 1, k - 1, :]
                link(tt(s2[:], r, r, ALU.mult))
                link(tt(s4[:], i, i, ALU.mult))
                link(tt(pw[:, 0, k, :], s2[:], s4[:], ALU.subtract))
                link(dve.scalar_tensor_tensor(out=pw[:, 1, k, :], in0=r, scalar=2.0, in1=i, op0=ALU.mult, op1=ALU.mult))
            dve.sem_inc(E["powers"], 1)
            dve.wait_ge(E["exps"], 2)
            link(tt(ab_re[:], mag[:], pw[:, 0, 0, :], ALU.mult))
            link(tt(ab_im[:], mag[:], sn[:], ALU.mult))
            link(dve.tensor_scalar(nr[:], ab_re[:], -1.0, None, ALU.add))
            link(tt(f_re[:], nr[:], a_re[:], ALU.mult))
            link(tt(f_im[:], ab_im[:], a_im[:], ALU.mult))
            link(tt(f_re[:], f_re[:], f_im[:], ALU.add))
            link(tt(f_re[:], f_re[:], t1[:], ALU.mult))
            link(tt(f_im[:], ab_im[:], a_re[:], ALU.mult))
            link(tt(t0[:], nr[:], a_im[:], ALU.mult))
            link(tt(f_im[:], f_im[:], t0[:], ALU.subtract))
            link(tt(f_im[:], f_im[:], t1[:], ALU.mult))
            fr, fi = (f[:].unsqueeze(2).broadcast_to([P, NT_ST, GRP_CH]) for f in (f_re, f_im))
            dve.wait_ge(E["zeroed"], 2)

            def own_channels(pad, j, r):
                p = slice(STATE * r, STATE * r + STATE)
                return pad[p, j].rearrange("p u (v n) -> p u v n", n=STEP)[:, :, :, GRP_CH * r:GRP_CH * r + GRP_CH]

            split = lambda a, r: a[STATE * r:STATE * r + STATE].rearrange("p (u v) n -> p u v n", v=4)
            for j, (x0, x1, op) in enumerate(((0, 1, ALU.subtract), (1, 0, ALU.add))):
                link(tt(bt[:, 0], b_in[:, x0], fr, ALU.mult))
                link(tt(bt[:, 1], b_in[:, x1], fi, ALU.mult))
                for r in range(2):
                    for u in range(4):
                        link(tt(own_channels(b_pad, j, r)[:, u], split(bt[:, 0], r)[:, u], split(bt[:, 1], r)[:, u], op))
            for j, (part, sign) in enumerate(((0, 1.0), (0, -1.0), (1, -1.0))):
                for r in range(2):
                    for u in range(4):
                        link(dve.tensor_scalar(own_channels(c_pad, j, r)[:, u], split(c_in[:, part], r)[:, u], sign, None,
                                               ALU.mult))
            dve.sem_inc(E["padded"], 1)

            for n in range(NT_ST):
                u, v, b = n // 4, n % 4, n % 2
                co, si = tab[:, u % 2, 0, v, :], tab[:, u % 2, 1, v, :]
                if v == 0:
                    dve.wait_ge(E["table_ready"], u + 1)
                dve.wait_ge(E["bu_ready"], n + 1)
                br, bi = bu[:, b, 0, :], bu[:, b, 1, :]
                tt(m[:, 0, :], br, co, ALU.mult)
                tt(m[:, 1, :], bi, si, ALU.mult)
                tt(m[:, 2, :], bi, co, ALU.mult)
                tt(m[:, 3, :], br, si, ALU.mult).then_inc(E["rot_done"], 1)
                dve.wait_ge(E["rot_done"], n + 1)
                tt(w[:, 0, :], m[:, 0, :], m[:, 1, :], ALU.add)
                link(tt(w[:, 1, :], m[:, 2, :], m[:, 3, :], ALU.subtract))
                decay = mag[:, n:n + 1].broadcast_to([P, SEQ])
                dve.tensor_tensor_scan(g[:, 0, :], decay, w[:, 0, :], 0.0, ALU.mult, ALU.add)
                link(dve.tensor_tensor_scan(g[:, 1, :], decay, w[:, 1, :], 0.0, ALU.mult, ALU.add))
                if n >= 2:
                    dve.wait_ge(E["y_done"], n - 1)
                for j, (x0, x1) in enumerate(((0, co), (1, si), (0, si), (1, co))):
                    ins = tt(zb[:, b, j, :], g[:, x0, :], x1, ALU.mult)
                ins.then_inc(E["z_ready"], 1)
                dve.wait_ge(E["z_ready"], n + 1)
                tt(last_h[:, 0, n:n + 1], zb[:, b, 0, SEQ - 1:SEQ], zb[:, b, 1, SEQ - 1:SEQ], ALU.subtract)
                tt(last_h[:, 1, n:n + 1], zb[:, b, 2, SEQ - 1:SEQ], zb[:, b, 3, SEQ - 1:SEQ], ALU.add).then_inc(E["ysum"], 1)
                if v == 3:
                    dve.wait_ge(E["y_done"], n + 1)
                    dve.scalar_tensor_tensor(out=S.uT[:, u, 0:SEQ], in0=S.uT[:, u, 0:SEQ], scalar=skip[:, u:u + 1],
                                             in1=yp[:, u % 2, :], op0=ALU.mult, op1=ALU.add).then_inc(E["y_ready"], 1)
            dve.wait_ge(E["bus_ready"], 1)
            bv = bus[:, 0:2 * NT_ST * NB].rearrange("p (j t b) -> p j t b", j=2, t=NT_ST)
            ar, ai = (a[:].unsqueeze(2).broadcast_to([P, NT_ST, NB]) for a in (ab_re, ab_im))
            for j, (x0, x1, op) in enumerate(((0, 1, ALU.subtract), (1, 0, ALU.add))):
                link(tt(ht[:, 0], h0[:, x0], ar, ALU.mult))
                link(tt(ht[:, 1], h0[:, x1], ai, ALU.mult))
                link(tt(hn[:, j], ht[:, 0], ht[:, 1], op))
                link(tt(hn[:, j], hn[:, j], bv[:, j], ALU.add))
            dve.sem_inc(E["hn_ready"], 1)
            dve.wait_ge(E["ys_done"], 1)
            link(tt(y[:, 0, 0:4 * NB].rearrange("p (u b) -> p u b", b=NB), S.uT[:, :, SEQ:TOK],
                    skip[:].unsqueeze(2).broadcast_to([P, 4, NB]), ALU.mult))
            tt(y[:, 1, 0:4 * NB], y[:, 0, 0:4 * NB], yps[:, 0:4 * NB], ALU.add).then_inc(E["hs_kept"], 1)

        @block.tensor
        def _(pe):
            pe.wait_ge(E["padded"], 1)
            for n in range(8):
                if n >= 4:
                    pe.wait_ge(E["b_kept"], n - 3)
                j = n // 4
                for v in range(4):
                    last = pe.transpose(bu[:, (n % 4) // 2, n % 2, P * v:P * v + P], b_pad[:, j, n % 4, P * v:P * v + P],
                                        S.ident[:])
                last.then_inc(E["b_done"], 1)
            pe.wait_ge(E["b_kept"], 8)
            for n in range(NT_ST):
                for j in range(2):
                    c = NT_ST * j + n
                    last = pe.matmul(bus[:, NB * c:NB * c + NB], bT[:, j, n, :], S.uT[:, n // 4, SEQ:TOK],
                                     start=True, stop=True)
            last.then_inc(E["bus_ready"], 1)

            def inputs(n):
                if n >= 2:
                    pe.wait_ge(E["rot_done"], n - 1)
                for j in range(2):
                    last = pe.matmul(bu[:, n % 2, j, :], bT[:, j, n, :], S.uT[:, n // 4, 0:SEQ], start=True, stop=True)
                last.then_inc(E["bu_ready"], 1)

            inputs(0)
            for n in range(NT_ST):
                u, v, b = n // 4, n % 4, n % 2
                if n + 1 < NT_ST:
                    inputs(n + 1)
                pe.wait_ge(E["z_ready"], n + 1)
                if v == 0 and u >= 2:
                    pe.wait_ge(E["y_ready"], u - 1)
                for j, c in enumerate((0, 1, 2, 2)):
                    last = pe.matmul(yp[:, u % 2, :], c_pad[:, c, u, P * v:P * v + P], zb[:, b, j, :],
                                     start=(v == 0 and j == 0), stop=(v == 3 and j == 3))
                last.then_inc(E["y_done"], 1)
            pe.wait_ge(E["hn_ready"], 1)
            for u in range(4):
                for v in range(4):
                    for j, c in enumerate((0, 2)):
                        last = pe.matmul(yps[:, NB * u:NB * u + NB], c_pad[:, c, u, P * v:P * v + P], hn[:, j, 4 * u + v, :],
                                         start=(v == 0 and j == 0), stop=(v == 3 and j == 1))
            last.then_inc(E["ys_done"], 1)


def stage_merge(nc, io, S):
    KA = 4
    with ExitStack() as ctx:
        sb = lambda n, s, d=F32: ctx.enter_context(nc.sbuf_tensor("me_" + n, s, d))
        sems = []
        sem = lambda n: new_semaphore(nc, ctx, sems, "me_" + n)
        w = sb("w", [P, 2, 3, KA, CHUNK])
        sig = sb("sig", [P, 2, HALF])
        t0 = sb("t0", [P, 2, HALF])
        t1 = sb("t1", [P, 2, HALF])
        ps = ctx.enter_context(nc.psum_tensor("me_ps", [P, 2, 3, 512], F32))
        landed = [sem("landed0"), sem("landed1")]
        done, sig_ready, merged, own_s = sem("done"), sem("sig_ready"), sem("merged"), sem("own")
        groups = [(m, h) for m in range(KT) for h in range(2)]
        block = open_block(nc, ctx, sems)

        @block.sync
        def _(sp):
            att = io["w_att_proj"].rearrange("a (k p) n -> p (a k) n", p=P)
            glu = io["w_ssm_glu"].rearrange("a (k p) n -> p (a k) n", p=P)
            for j in range(2):
                c = CHUNK * j
                for i, src in enumerate((att[:, :, c:c + CHUNK], glu[:, :, c:c + CHUNK], glu[:, :, D + c:D + c + CHUNK])):
                    sp.dma_start(w[:, j, i], src).then_inc(landed[j], 16)

        @block.tensor
        def _(pe):
            for n, (m, h) in enumerate(groups):
                if n % 8 == 0:
                    pe.wait_ge(landed[n // 8], 48)
                if n >= 2:
                    pe.wait_ge(merged, n - 1)
                for i, x in enumerate((S.oT, S.uT, S.uT)):
                    for k in range(KA):
                        last = pe.matmul(ps[:, n % 2, i, 0:HALF], w[:, m // 4, i, k, P * (m % 4):P * (m % 4) + P],
                                         x[:, k, HALF * h:HALF * h + HALF], start=(k == 0), stop=(k == KA - 1))
                last.then_inc(done, 1)

        @block.scalar
        def _(act):
            for n, (m, h) in enumerate(groups):
                act.wait_ge(done, n + 1)
                if n >= 2:
                    act.wait_ge(merged, n - 1)
                act.activation(sig[:, n % 2, :], ps[:, n % 2, 2, 0:HALF], ACT.Sigmoid).then_inc(sig_ready, 1)

        @block.vector
        def _(dve):
            link = own(dve, own_s)
            for n, (m, h) in enumerate(groups):
                b = n % 2
                tok = slice(HALF * h, HALF * h + HALF)
                dve.wait_ge(done, n + 1)
                dve.tensor_tensor(t0[:, b, :], ps[:, b, 0, 0:HALF], S.sgT[:, m, tok], ALU.mult)
                dve.wait_ge(sig_ready, n + 1)
                link(dve.tensor_tensor(t1[:, b, :], ps[:, b, 1, 0:HALF], sig[:, b, :], ALU.mult))
                link(dve.tensor_tensor(t1[:, b, :], t1[:, b, :], S.sgT[:, KT + m, tok], ALU.mult))
                dve.tensor_tensor(S.sgT[:, m, tok], t0[:, b, :], t1[:, b, :], ALU.add).then_inc(merged, 1)


def stage_output(nc, io, S):
    with ExitStack() as ctx:
        sb = lambda n, s, d=F32: ctx.enter_context(nc.sbuf_tensor("ou_" + n, s, d))
        sems = []
        sem = lambda n: new_semaphore(nc, ctx, sems, "ou_" + n)
        w = sb("w", [P, 2, KT, CHUNK])
        gain = sb("gain", [P, D])
        junk = sb("junk", [P, D])
        ss = sb("ss", [P, TILES])
        rstd = sb("rstd", [P, TILES])
        h = S.h
        ps = ctx.enter_context(nc.psum_tensor("ou_ps", [P, 4, 512], F32))
        pt = ctx.enter_context(nc.psum_tensor("ou_pt", [P, 2, 512], F32))
        landed = [sem("landed0"), sem("landed1")]
        names = ("x", "padz", "done", "added", "sq", "var", "root", "normed", "own", "tr", "hT", "gain")
        E = {n: sem(n) for n in names}
        block = open_block(nc, ctx, sems)

        @block.gpsimd
        def _(pool):
            pool.memset(S.y1[:, 4, :], 0.0).then_inc(E["padz"], 1)

        @block.sync
        def _(sp):
            src = io["w_out"].rearrange("a (k p) n -> p (a k) n", p=P)
            sp.dma_start(w[:, 0], src[:, :, 0:CHUNK]).then_inc(landed[0], 16)
            sp.dma_start(w[:, 1], src[:, :, CHUNK:D]).then_inc(landed[1], 16)
            sp.dma_start(S.y1[:, 0:4, :], io["x_prompt"].rearrange("a (t p) n -> p (a t) n", p=P)).then_inc(E["x"], 16)
            sp.wait_ge(E["padz"], 1)
            sp.dma_start(S.y1[0:NB, 4, :], io["x_sample"].rearrange("b a n -> (b a) n")).then_inc(E["x"], 16)
            sp.dma_start(gain[:], io["norm_ffn"][0, :].partition_broadcast(P)).then_inc(E["gain"], 16)

        @block.tensor
        def _(pe):
            def turn(t):
                pe.wait_ge(E["normed"], t + 1)
                for j in (2 * t, 2 * t + 1):
                    if j >= 2:
                        pe.wait_ge(E["hT"], j - 1)
                    for k in range(4):
                        c = P * (4 * (j % 2) + k)
                        last = pe.transpose(pt[:, j % 2, P * k:P * k + P], h[:, t, c:c + P], S.ident[:])
                    last.then_inc(E["tr"], 1)

            n = 0
            for t in range(TILES):
                for c in range(2):
                    if t == 0:
                        pe.wait_ge(landed[c], 16)
                    if n >= 4:
                        pe.wait_ge(E["added"], n - 3)
                    for k in range(KT):
                        last = pe.matmul(ps[0:rows(t), n % 4, :], S.sgT[:, k, P * t:P * t + rows(t)], w[:, c, k, :],
                                         start=(k == 0), stop=(k == KT - 1))
                    last.then_inc(E["done"], 1)
                    n += 1
                if t:
                    turn(t - 1)
            turn(TILES - 1)

        @block.vector
        def _(dve):
            link = own(dve, E["own"])
            dve.wait_ge(E["x"], 32)
            dve.wait_ge(E["gain"], 16)
            for n in range(2 * TILES):
                t, c = divmod(n, 2)
                y = S.y1[0:rows(t), t, CHUNK * c:CHUNK * c + CHUNK]
                dve.wait_ge(E["done"], n + 1)
                dve.tensor_tensor(y, ps[0:rows(t), n % 4, :], y, ALU.add).then_inc(E["added"], 1)
                if c:
                    norm_tile(dve, link, t, h, S.y1, gain, ss, rstd, E["sq"], E["var"], E["root"], E["normed"])

        @block.scalar
        def _(act):
            for t in range(TILES):
                act.wait_ge(E["added"], 2 * t + 2)
                square_tile(act, t, S.y1, junk, ss, rstd, E["sq"], E["var"], E["root"])
                for j in (2 * t, 2 * t + 1):
                    act.wait_ge(E["tr"], j + 1)
                    act.activation(S.hT[:, 4 * (j % 2):4 * (j % 2) + 4, P * t:P * t + P],
                                   pt[:, j % 2, :].rearrange("p (k n) -> p k n", k=4), ACT.Copy).then_inc(E["hT"], 1)


class Chosen:

    def __init__(self, nc, ctx):
        sb = lambda n, s, d=F32: ctx.enter_context(nc.sbuf_tensor("ch_" + n, s, d))
        self.v = sb("v", [P, TILES, 2 * HEADS_P, TOPK])
        self.fi = sb("fi", [P, TILES, 2 * HEADS_P, TOPK])
        self.cand = sb("cand", [P, HEADS_P, TOPK, TOPK])
        self.hit = sb("hit", [P, HEADS_P, TOPK, TOPK])
        self.sc = sb("sc", [P, HEADS_P, TOPK])
        self.ci = sb("ci", [P, HK], U32)
        self.hl = sb("hl", [P, 2, HK], U32)
        self.hf = sb("hf", [P, 2, HK])
        self.pick = sb("pick", [P, 2, HK])
        self.iota = sb("iota", [P, TOPK])
        self.den = sb("den", [P, HEADS_P])
        self.eg = sb("eg", [P, 2, HK])


def best16(dve, link, places):
    for r in range(2):
        part = slice(8 * r, 8 * r + 8)
        for vals, idx, x in places:
            ins = dve.max(vals[:, part], x)
        link(ins)
        for vals, idx, x in places:
            ins = dve.max_index(idx[:, part], vals[:, part], x)
        link(ins)
        if r == 0:
            for vals, idx, x in places:
                ins = dve.match_replace(x, vals[:, part], x, LOW)
            link(ins)


def choose(dve, link, R, t, first, count, shifted):
    v, f = (x[:, t].rearrange("p (h w) a -> p h w a", w=2)[:, bass.ds(first, count)] for x in (R.v, R.fi))
    cand, sc, hit = R.cand[:, 0:count], R.sc[:, 0:count], R.hit[:, 0:count]
    ci, hl, hf, pick = R.ci[:, 0:count * TOPK], R.hl, R.hf, R.pick
    n = count * TOPK
    cube = [P, count, TOPK, TOPK]
    to = [R.eg[:, j, bass.ds(first * TOPK, n)] for j in range(2)]
    link(dve.tensor_tensor(cand, v[:, :, 0, :].unsqueeze(3).broadcast_to(cube),
                           v[:, :, 1, :].unsqueeze(2).broadcast_to(cube), ALU.add))
    best16(dve, link, [(R.sc[:, h, :], R.ci[:, TOPK * h:TOPK * h + TOPK], R.cand[:, h].rearrange("p a b -> p (a b)"))
                       for h in range(count)])
    dve.tensor_tensor(to[1].rearrange("p (h k) -> p h k", k=TOPK), sc, sc[:, :, 0:1].broadcast_to([P, count, TOPK]),
                      ALU.subtract).then_inc(shifted, 1)
    dve.tensor_scalar(hl[:, 0, 0:n], ci, 4, None, ALU.logical_shift_right)
    link(dve.tensor_scalar(hl[:, 1, 0:n], ci, TOPK - 1, None, ALU.bitwise_and))
    link(dve.tensor_copy(hf[:, :, 0:n], hl[:, :, 0:n]))
    for j in range(2):
        link(dve.tensor_tensor(hit.rearrange("p h k a -> p (h k) a"),
                               hf[:, j, 0:n].unsqueeze(2).broadcast_to([P, n, TOPK]),
                               R.iota[:].unsqueeze(1).broadcast_to([P, n, TOPK]), ALU.is_equal))
        link(dve.tensor_tensor(hit, hit, f[:, :, j, :].unsqueeze(2).broadcast_to(cube), ALU.mult))
        link(dve.tensor_reduce(pick[:, j, 0:n], hit.rearrange("p h k a -> p (h k) a"), AX_X, ALU.add))
    link(dve.scalar_tensor_tensor(out=to[0], in0=pick[:, 0, 0:n], scalar=float(NKEYS), in1=pick[:, 1, 0:n],
                                  op0=ALU.mult, op1=ALU.add))


def normalise(dve, link, R, first, count, ready):
    g = R.eg[:, 1, bass.ds(first * TOPK, count * TOPK)].rearrange("p (h k) -> p h k", k=TOPK)
    den = R.den[:, 0:count]
    link(dve.tensor_reduce(den, g, AX_X, ALU.add))
    link(dve.reciprocal(den, den))
    dve.tensor_tensor(g, g, den.unsqueeze(2).broadcast_to([P, count, TOPK]), ALU.mult).then_inc(ready, 1)


def turn_choice(pe, S, done, bank):
    for j in range(2):
        last = pe.transpose(bank[:, P * j:P * j + P], S.R.eg[:, j, :], S.ident[:])
    last.then_inc(done, 1)


def keep_choice(act, S, t, kept, bank):
    n = rows(t)
    act.activation(S.idxT[:, P * t:P * t + n], bank[:, 0:n], ACT.Copy).then_inc(kept, 1)
    act.activation(S.gateT[:, P * t:P * t + n], bank[:, P:P + n], ACT.Copy).then_inc(kept, 1)


def stage_route(nc, io, S):
    HH = 2 * HEADS_P
    with ExitStack() as ctx:
        sb = lambda n, s, d=F32: ctx.enter_context(nc.sbuf_tensor("ro_" + n, s, d))
        sems = []
        sem = lambda n: new_semaphore(nc, ctx, sems, "ro_" + n)
        w = sb("w", [P, 2, KT, CHUNK])
        keys = sb("keys", [P, 2, NKEYS])
        q = sb("q", [P, 2, PAD])
        s = sb("s", [P, TILES, HH, NKEYS])
        iu = sb("iu", [P, TILES, HH, TOPK], U32)
        rest = sb("rest", [P, 2, D])
        part = sb("part", [P, 2, 3, D], BF16)
        R, h = S.R, S.h
        pq = ctx.enter_context(nc.psum_tensor("ro_pq", [P, 2, 2, 512], F32))
        pss = ctx.enter_context(nc.psum_tensor("ro_ps", [P, 2, 2, 512], F32))
        wl = [sem("landed0"), sem("landed1")]
        stored = [sem("stored0"), sem("stored1")]
        names = ("keys", "qz", "q_done", "q_kept", "s_done", "s_kept", "own", "iota", "shifted", "exped", "eg_ready",
                 "eg_done", "eg_kept", "hi", "r1", "mid", "lo")
        E = {n: sem(n) for n in names}
        block = open_block(nc, ctx, sems)

        @block.gpsimd
        def _(pool):
            pool.memset(q[:, :, TOK:PAD], 0.0).then_inc(E["qz"], 1)
            pool.memset(S.idxT[:, TOK:], 0.0).then_inc(E["qz"], 1)
            pool.iota(R.iota[:], [[1, TOPK]], base=0, channel_multiplier=0,
                      allow_small_or_imprecise_dtypes=True).then_inc(E["iota"], 1)
            for t in range(TILES):
                b = t % 2
                pool.wait_ge(E["hi"], t + 1)
                if t >= 2:
                    pool.wait_ge(E["lo"], t - 1)
                pool.tensor_tensor(rest[:, b, :], S.h[:, t, :], part[:, b, 0, :], ALU.subtract).then_inc(E["r1"], 1)
                pool.wait_ge(E["mid"], t + 1)
                pool.tensor_tensor(part[:, b, 2, :], rest[:, b, :], part[:, b, 1, :], ALU.subtract).then_inc(E["lo"], 1)

        @block.sync
        def _(sp):
            src = io["peer_w_q"].rearrange("a (k p) n -> p (a k) n", p=P)
            sp.dma_start(keys[:, 0], io["k1T"]).then_inc(E["keys"], 16)
            sp.dma_start(keys[:, 1], io["k2T"]).then_inc(E["keys"], 16)
            for c in range(4):
                if c >= 2:
                    sp.wait_ge(E["q_done"], 8 * (c - 1))
                sp.dma_start(w[:, c % 2], src[:, :, CHUNK * c:CHUNK * c + CHUNK]).then_inc(wl[c % 2], 16)
            for t in range(TILES):
                b = t % 2
                sp.wait_ge(E["lo"], t + 1)
                sp.dma_start(S.h_split[P * t:P * t + rows(t)].rearrange("p j n -> p (j n)"),
                             part[0:rows(t), b].rearrange("p j n -> p (j n)")).then_inc(stored[b], 16)
            sp.wait_ge(stored[0], 48)
            sp.wait_ge(stored[1], 32)

        @block.tensor
        def _(pe):
            pe.wait_ge(E["keys"], 32)
            pe.wait_ge(E["qz"], 2)

            def queries(hh):
                c, m = divmod(hh, 4)
                if m == 0:
                    pe.wait_ge(wl[c % 2], 16 * (c // 2 + 1))
                if hh >= 2:
                    pe.wait_ge(E["q_kept"], 2 * (hh - 1))
                for h in range(2):
                    for k in range(KT):
                        last = pe.matmul(pq[:, hh % 2, h, 0:HALF], w[:, c % 2, k, P * m:P * m + P],
                                         S.hT[:, k, HALF * h:HALF * h + HALF], start=(k == 0), stop=(k == KT - 1))
                    last.then_inc(E["q_done"], 1)

            queries(0)
            for hh in range(HH):
                if hh + 1 < HH:
                    queries(hh + 1)
                pe.wait_ge(E["q_kept"], 2 * hh + 2)
                if hh >= 2:
                    pe.wait_ge(E["s_kept"], 2 * (hh - 1))
                for t in range(TILES):
                    last = pe.matmul(pss[:, hh % 2, t // 4, P * (t % 4):P * (t % 4) + P], q[:, hh % 2, P * t:P * t + P],
                                     keys[:, hh % 2, :], start=True, stop=True)
                last.then_inc(E["s_done"], 1)
            pe.wait_ge(E["eg_ready"], 1)
            turn_choice(pe, S, E["eg_done"], pq[:, 0, 0, 0:2 * P])

        @block.scalar
        def _(act):
            copy = lambda to, of: act.activation(to, of, ACT.Copy)

            def split_tile(t):
                b = t % 2
                if t >= 2:
                    act.wait_ge(stored[b], 16 * (t // 2))
                copy(part[:, b, 0, :], S.h[:, t, :]).then_inc(E["hi"], 1)
                act.wait_ge(E["r1"], t + 1)
                copy(part[:, b, 1, :], rest[:, b, :]).then_inc(E["mid"], 1)

            def keep_scores(hh):
                act.wait_ge(E["s_done"], hh + 1)
                copy(s[:, 0:4, hh, :], pss[:, hh % 2, 0, :].rearrange("p (t n) -> p t n", t=4)).then_inc(E["s_kept"], 1)
                copy(s[:, 4, hh, :], pss[:, hh % 2, 1, 0:NKEYS]).then_inc(E["s_kept"], 1)
            for hh in range(HH):
                for h in range(2):
                    act.wait_ge(E["q_done"], 2 * hh + h + 1)
                    if hh >= 2:
                        act.wait_ge(E["s_done"], hh - 1)
                    copy(q[:, hh % 2, HALF * h:HALF * h + HALF], pq[:, hh % 2, h, 0:HALF]).then_inc(E["q_kept"], 1)
                if hh:
                    keep_scores(hh - 1)
                if hh % 3 == 0 and hh // 3 < TILES:
                    split_tile(hh // 3)
            keep_scores(HH - 1)
            act.wait_ge(E["shifted"], 1)
            act.activation(R.eg[:, 1, :], R.eg[:, 1, :], ACT.Exp).then_inc(E["exped"], 1)
            act.wait_ge(E["eg_done"], 1)
            keep_choice(act, S, 0, E["eg_kept"], pq[:, 0, 0, 0:2 * P])

        @block.vector
        def _(dve):
            link = own(dve, E["own"])

            for hh in range(HH):
                dve.wait_ge(E["s_kept"], 2 * hh + 2)
                best16(dve, link, [(R.v[:, t, hh, :], iu[:, t, hh, :], s[:, t, hh, :]) for t in range(TILES)])
            link(dve.tensor_copy(R.fi[:], iu[:]))
            dve.wait_ge(E["iota"], 1)
            choose(dve, link, R, 0, 0, HEADS_P, E["shifted"])
            dve.wait_ge(E["exped"], 1)
            normalise(dve, link, R, 0, HEADS_P, E["eg_ready"])


def stage_experts(nc, io, S):
    GROUP, SUB, PER = 10, 5, 20
    TURNS = TOK // PER
    assert TURNS * PER == TOK
    with ExitStack() as ctx:
        sb = lambda n, s, d=F32: ctx.enter_context(nc.sbuf_tensor("ex_" + n, s, d))
        ps = lambda n, s: ctx.enter_context(nc.psum_tensor("ex_" + n, s, F32))
        sems = []
        sem = lambda n: new_semaphore(nc, ctx, sems, "ex_" + n)
        ug = sb("ug", [P, GROUP, D])
        vg = sb("vg", [P, GROUP, D])
        h_rows = sb("h_rows", [3 * GROUP, 2, D], BF16)
        spread = sb("spread", [3 * GROUP, GROUP, P], BF16)
        stage = sb("stage", [P, PER], U32)
        dots = sb("dots", [P, PER])
        gelu = sb("gelu", [P, PER])
        wts = sb("wts", [P, 2, GROUP * GROUP])
        out_rows = sb("out_rows", [GROUP, 2, D])
        hb = [ps("hb0", [P, D]), ps("hb1", [P, D])]
        acc = [ps("acc0", [P, D]), ps("acc1", [P, D])]
        wts_zero, spread_ready, paced = sem("wts_zero"), sem("spread_ready"), sem("paced")
        rows_landed = [sem(f"rows_landed{g}") for g in range(2)]
        staged, hb_ready, dot_done = sem("staged"), sem("hb_ready"), sem("dot_done")
        gelu_done, wts_ready, v_used, acc_kept = sem("gelu_done"), sem("wts_ready"), sem("v_used"), sem("acc_kept")
        stored = [sem(f"stored{g}") for g in range(2)]
        names = ("own", "shifted", "exped", "turned", "eg_ready", "eg_done", "eg_kept")
        E = {n: sem(n) for n in names}
        u_landed = [sem(f"u_landed{k}") for k in range(GROUP)]
        v_landed = [sem(f"v_landed{k}") for k in range(GROUP)]
        u_tab, v_tab = (io[n].rearrange("a e n -> (a e) n") for n in ("peer_u", "peer_v"))
        h_split = S.h_split.rearrange("n j d -> (n j) d")
        R = S.R
        CHOOSING = HEADS_P // 2
        SPAN = CHOOSING + 1
        assert all(SPAN * t <= (P * t - PER - 2 * SUB) // PER + 1 for t in range(1, TILES))
        DOTS0, USED0, SPREAD0, KEPT0, STORED0 = GROUP, PER, PER, 2, 16
        block = open_block(nc, ctx, sems)

        @block.gpsimd
        def _(pool):
            for counter, value in ((dot_done, DOTS0), (v_used, USED0), (hb_ready, SPREAD0), (acc_kept, KEPT0),
                                   (stored[0], STORED0), (stored[1], STORED0)):
                pool.sem_inc(counter, value)
            pool.memset(wts[:], 0.0).then_inc(wts_zero, 1)
            pool.memset(spread[:], 1.0).then_inc(spread_ready, 1)
            pool.wait_ge(spread_ready, 1)
            pool.affine_select(out=spread[:], in_=spread[:], pattern=[[-3, GROUP], [0, P]], compare_op=ALU.is_ge,
                               fill=0.0, base=0, channel_multiplier=1).then_inc(spread_ready, 1)
            pool.wait_ge(spread_ready, 2)
            pool.affine_select(out=spread[:], in_=spread[:], pattern=[[3, GROUP], [0, P]], compare_op=ALU.is_ge,
                               fill=0.0, base=2, channel_multiplier=-1).then_inc(spread_ready, 1)

            def gather(to, table, t, landed):
                pool.sem_inc(paced, 1)
                pool.indirect_dma_start(to[:, t % GROUP, :], None, table,
                                        bass.IndirectOffsetOnAxis(ap=stage[:, t:t + 1], axis=0))\
                    .then_inc(landed[t % GROUP], 16)

            with pool.Fori(0, TURNS) as i:
                for q in range(PER // SUB):
                    pool.wait_ge(staged, i * 4 + q + 1)
                    for t in range(SUB * q, SUB * q + SUB):
                        pool.wait_ge(dot_done, i * PER + t + 1)
                        gather(ug, u_tab, t, u_landed)
                    for t in range(SUB * q, SUB * q + SUB):
                        pool.wait_ge(v_used, i * PER + t + 1 + USED0 - GROUP)
                        gather(vg, v_tab, t, v_landed)

        @block.sync
        def _(sp):
            with sp.Fori(0, TURNS) as i:
                for g in range(2):
                    sp.wait_ge(hb_ready, i * PER + GROUP * g + GROUP)
                    sp.dma_start(h_rows[:, g, :], h_split[bass.ds(i * (3 * PER) + 3 * GROUP * g, 3 * GROUP), :])\
                      .then_inc(rows_landed[g], 16)

        @block.tensor
        def _(pe):
            pe.wait_ge(spread_ready, 3)
            pe.wait_ge(wts_zero, 1)

            def broadcast(i, t):
                if t % GROUP == 0:
                    pe.wait_ge(rows_landed[t // GROUP], i * 16 + 16)
                pe.wait_ge(dot_done, i * PER + t - 1 + DOTS0)
                for h in range(2):
                    last = pe.matmul(hb[t % 2][:, CHUNK * h:CHUNK * h + CHUNK], spread[:, t % GROUP, :],
                                     h_rows[:, t // GROUP, CHUNK * h:CHUNK * h + CHUNK], start=True, stop=True)
                last.then_inc(hb_ready, 1)

            def combine(i, t):
                g, k = divmod(t, GROUP)
                if t % SUB == 0:
                    pe.wait_ge(wts_ready, i * 4 + t // SUB + 1)
                if k == 0:
                    pe.wait_ge(acc_kept, i * 2 + g + 1)
                pe.wait_ge(v_landed[k], i * 32 + 16 * g + 16)
                for h in range(2):
                    last = pe.matmul(acc[g][0:GROUP, CHUNK * h:CHUNK * h + CHUNK], wts[:, g, GROUP * k:GROUP * k + GROUP],
                                     vg[:, k, CHUNK * h:CHUNK * h + CHUNK], start=(k == 0), stop=(k == GROUP - 1))
                last.then_inc(v_used, 1)

            def turn(i, last_turn):
                for t in range(PER):
                    if t < PER - SUB:
                        broadcast(i, t + SUB)
                    elif not last_turn:
                        broadcast(i + 1, t + SUB - PER)
                    combine(i, t)

            for t in range(SUB):
                broadcast(0, t)
            for n in range(1, TILES):
                first = SPAN * (n - 1)
                with pe.Fori(first, first + CHOOSING) as i:
                    turn(i, False)
                pe.wait_ge(E["eg_ready"], CHOOSING * n)
                pe.wait_ge(acc_kept, 2 * (first + CHOOSING) - 1 + KEPT0)
                turn_choice(pe, S, E["eg_done"], acc[0][:, 0:2 * P])
                pe.wait_ge(E["eg_kept"], 2 * n)
                turn(first + CHOOSING, False)
            with pe.Fori(SPAN * (TILES - 1), TURNS - 1) as i:
                turn(i, False)
            turn(TURNS - 1, True)

        @block.vector
        def _(dve):
            for q in range(2):
                dve.tensor_copy(stage[:, SUB * q:SUB * q + SUB], S.idxT[:, SUB * q:SUB * q + SUB]).then_inc(staged, 1)

            def turn(i, tile=None):
                if tile:
                    dve.sem_clear(E["own"])
                    link = own(dve, E["own"])
                for q in range(PER // SUB):
                    g = q // 2
                    t0 = SUB * q
                    dve.wait_ge(v_used, i * PER + t0 - SUB + USED0)
                    c = (t0 + 2 * SUB) % PER
                    dve.tensor_copy(stage[:, c:c + SUB], S.idxT[:, bass.ds(i * PER + t0 + 2 * SUB, SUB)]).then_inc(staged, 1)
                    for t in range(t0, t0 + SUB):
                        dve.wait_ge(u_landed[t % GROUP], i * 32 + 16 * (t // GROUP) + 16)
                        dve.wait_ge(hb_ready, i * PER + t + 1 + SPREAD0)
                        rows_ = ug[:, t % GROUP, :]
                        dve.scalar_tensor_tensor(out=rows_, in0=rows_, scalar=1.0, in1=hb[t % 2][:], op0=ALU.mult,
                                                 op1=ALU.mult, accum_out=dots[:, t:t + 1]).then_inc(dot_done, 1)
                    dve.wait_ge(gelu_done, i * 4 + q + 1)
                    first = (GROUP + 1) * SUB * (q % 2)
                    dve.tensor_tensor(wts[:, g, first:first + (GROUP + 1) * (SUB - 1) + 1:GROUP + 1],
                                      gelu[:, t0:t0 + SUB], S.gateT[:, bass.ds(i * PER + t0, SUB)],
                                      ALU.mult).then_inc(wts_ready, 1)
                    if tile and q < 2:
                        choose(dve, link, R, tile, i * 2 + (q - 2 * SPAN * (tile - 1)), 1, E["shifted"])
                if tile:
                    dve.wait_ge(E["exped"], i + (2 - tile))
                    dve.sem_inc(E["turned"], 1)
                    normalise(dve, link, R, i * 2 - 2 * SPAN * (tile - 1), 2, E["eg_ready"])

            for n in range(1, TILES):
                first = SPAN * (n - 1)
                with dve.Fori(first, first + CHOOSING) as i:
                    turn(i, n)
                turn(first + CHOOSING)
                dve.wait_ge(E["eg_kept"], 2 * n)
            with dve.Fori(SPAN * (TILES - 1), TURNS) as i:
                turn(i)

        @block.scalar
        def _(act):
            def turn(i, tile=None):
                for q in range(PER // SUB):
                    t0 = SUB * q
                    if tile and q == 3:
                        act.wait_ge(E["shifted"], i * 2 + (2 - 2 * (tile - 1)))
                        two = R.eg[:, 1, bass.ds(i * (2 * TOPK) - 2 * TOPK * SPAN * (tile - 1), 2 * TOPK)]
                        act.activation(two, two, ACT.Exp).then_inc(E["exped"], 1)
                    act.wait_ge(dot_done, i * PER + t0 + SUB + DOTS0)
                    act.activation(gelu[:, t0:t0 + SUB], dots[:, t0:t0 + SUB], ACT.Gelu_apprx_tanh).then_inc(gelu_done, 1)
                    if q % 2:
                        g = q // 2
                        act.wait_ge(v_used, i * PER + t0 + SUB + USED0)
                        act.wait_ge(stored[g], i * 16 + STORED0)
                        act.activation(out_rows[:, g, :], acc[g][0:GROUP, :], ACT.Copy).then_inc(acc_kept, 1)
                        act.wait_ge(acc_kept, i * 2 + g + 1 + KEPT0)
                        act.dma_start(S.peer_out[bass.ds(i * PER + GROUP * g, GROUP), :], out_rows[:, g, :])\
                           .then_inc(stored[g], 16)

            for n in range(1, TILES):
                first = SPAN * (n - 1)
                with act.Fori(first, first + CHOOSING) as i:
                    turn(i, n)
                act.wait_ge(E["eg_done"], n)
                keep_choice(act, S, n, E["eg_kept"], acc[0][:, 0:2 * P])
                turn(first + CHOOSING)
            with act.Fori(SPAN * (TILES - 1), TURNS) as i:
                turn(i)
            for g in range(2):
                act.wait_ge(stored[g], 16 * TURNS + STORED0)


def stage_finish(nc, io, S):
    with ExitStack() as ctx:
        sb = lambda n, s, d=F32: ctx.enter_context(nc.sbuf_tensor("fi_" + n, s, d))
        sems = []
        sem = lambda n: new_semaphore(nc, ctx, sems, "fi_" + n)
        x = sb("x", [P, TILES, D])
        gain = sb("gain", [P, D])
        junk = sb("junk", [P, D])
        ss = sb("ss", [P, TILES])
        rstd = sb("rstd", [P, TILES])
        names = ("padz", "gain", "added", "sq", "var", "root", "normed", "own", "stored")
        E = {n: sem(n) for n in names}
        landed = [sem(f"landed{t}") for t in range(TILES)]
        block = open_block(nc, ctx, sems)

        @block.gpsimd
        def _(pool):
            pool.memset(x[:, 4, :], 0.0).then_inc(E["padz"], 1)

        @block.sync
        def _(sp):
            sp.dma_start(gain[:], io["norm_final"].partition_broadcast(P)).then_inc(E["gain"], 16)
            for t in range(4):
                sp.dma_start(x[:, t, :], S.peer_out[P * t:P * t + P]).then_inc(landed[t], 16)
            sp.wait_ge(E["padz"], 1)
            sp.dma_start(x[0:NB, 4, :], S.peer_out[SEQ:TOK]).then_inc(landed[4], 16)
            to = io["y_prompt"].rearrange("a (t p) n -> p (a t) n", p=P)
            for t in range(TILES):
                sp.wait_ge(E["normed"], t + 1)
                if t < 4:
                    sp.dma_start(to[:, t], x[:, t, :]).then_inc(E["stored"], 16)
                else:
                    sp.dma_start(io["y_sample"].rearrange("b a n -> (b a) n"), x[0:NB, 4, :]).then_inc(E["stored"], 16)
            sp.wait_ge(E["stored"], 16 * TILES)

        @block.vector
        def _(dve):
            link = own(dve, E["own"])
            dve.wait_ge(E["gain"], 16)
            for t in range(TILES):
                dve.wait_ge(landed[t], 16)
                dve.tensor_tensor(x[:, t, :], x[:, t, :], S.y1[:, t, :], ALU.add).then_inc(E["added"], 1)
                if t:
                    norm_tile(dve, link, t - 1, x, x, gain, ss, rstd, E["sq"], E["var"], E["root"], E["normed"])
            norm_tile(dve, link, TILES - 1, x, x, gain, ss, rstd, E["sq"], E["var"], E["root"], E["normed"])

        @block.scalar
        def _(act):
            for t in range(TILES):
                act.wait_ge(E["added"], t + 1)
                square_tile(act, t, x, junk, ss, rstd, E["sq"], E["var"], E["root"])


class Kept:
    pass


def build(nc, io):
    with ExitStack() as ctx:
        kb = lambda c, n, s, d=F32: c.enter_context(nc.sbuf_tensor(n, s, d))
        S = Kept()
        S.h_split = nc.dram_tensor("h_split", [TOK, 3, D], BF16).ap()
        S.peer_out = nc.dram_tensor("peer_out", [TOK, D], F32).ap()
        S.gather_sem = ctx.enter_context(nc.semaphore("gather_sem"))
        S.ident = kb(ctx, "ident", [P, P])
        with ExitStack() as c1:
            S.uT = kb(c1, "uT", [P, 4, TOK])
            S.sgT = kb(c1, "sgT", [P, 16, TOK])
            S.oT = kb(c1, "oT", [P, 4, TOK])
            with ExitStack() as c2:
                S.w1k, S.w1v = kb(c2, "w1k", [P, CMP_LEN, P]), kb(c2, "w1v", [P, CMP_LEN, P])
                S.w2k, S.w2v = kb(c2, "w2k", [P, P]), kb(c2, "w2v", [P, P])
                S.hbias = kb(c2, "hbias", [P, 2])
                S.qTs, S.kTs = kb(c2, "qTs", [P, REP, NB]), kb(c2, "kTs", [P, 2, NB])
                S.vs, S.vw = kb(c2, "vs", [NB, KVW]), kb(c2, "vw", [NB, KVW])
                S.gates_s = kb(c2, "gates_s", [NB, 3 * NH])
                with ExitStack() as c3:
                    S.z = kb(c3, "z", [P, TILES, NAT])
                    S.gates = kb(c3, "gates", [P, TILES, 3 * NH])
                    stage_project(nc, io, S)
                    stage_attend(nc, io, S)
                stage_decode(nc, io, S)
            stage_state_space(nc, io, S)
            stage_merge(nc, io, S)
            S.y1 = ctx.enter_context(nc.sbuf_tensor("y1", [P, TILES, D], F32, side="right"))
            S.hT = ctx.enter_context(nc.sbuf_tensor("hT", [P, KT, PAD], F32, side="right"))
            S.idxT = ctx.enter_context(nc.sbuf_tensor("idxT", [P, TOK + 10], U32, side="right"))
            S.gateT = ctx.enter_context(nc.sbuf_tensor("gateT", [P, TOK], F32, side="right"))
            S.h = ctx.enter_context(nc.sbuf_tensor("h", [P, TILES, D], F32, side="right"))
            stage_output(nc, io, S)
        with ExitStack() as c1:
            S.R = Chosen(nc, c1)
            stage_route(nc, io, S)
            stage_experts(nc, io, S)
        stage_finish(nc, io, S)


def host_constants():
    half = HD // 2
    inv = np.float32(10000.0) ** (-np.arange(half, dtype=np.float32) / np.float32(half))
    pos = np.zeros((PAD,), np.float32)
    pos[:SEQ] = np.arange(SEQ)
    pos[SEQ:TOK] = PAST
    ang = (pos[:, None] * inv[None, :]).astype(np.float32)
    lay = lambda a: np.ascontiguousarray(a.astype(np.float32).reshape(TILES, P, half).transpose(1, 0, 2))
    st = np.arange(NC_S)[:, None] * CMP_STRIDE
    ss = np.arange(NS_S)[None, :] * SEL_BLOCK
    touch = ((st <= ss + SEL_BLOCK - 1) & (st + CMP_LEN - 1 >= ss)).astype(np.float32)
    row = np.arange(NB * NH)
    return {
        "rope_cos": lay(np.cos(ang.astype(np.float64))), "rope_sin": lay(np.sin(ang.astype(np.float64))),
        "c_touch": touch,
        "c_same": (row[:, None] // REP == row[None, :] // REP).astype(np.float32),
        "c_seq": (row[:, None] // NH == np.arange(NB)[None, :]).astype(np.float32),
        "c_group": ((row[:, None] // REP) % NKV == np.arange(NKV)[None, :]).astype(np.float32),
    }


IN = ["x_prompt", "x_sample", "cache_k_cmp", "cache_v_cmp", "cache_k_sel", "cache_v_sel", "cache_k_win", "cache_v_win",
      "page_table", "norm_mix", "w_in", "cmp_w1_k", "cmp_w2_k", "cmp_w1_v", "cmp_w2_v", "w_att_proj", "w_ssm_glu",
      "w_out", "norm_ffn", "peer_w_q", "peer_u", "peer_v", "norm_final"]
KV = (1, 1, SEQ, NKV, HD)
SKV = (1, NB, 1, NKV, HD)
WKV = (1, NB, 512, NKV, HD)
OUT = [("y_prompt", (1, SEQ, D)), ("y_sample", (NB, 1, D)), ("p_k_cmp", KV), ("p_v_cmp", KV), ("p_k_sel", KV),
       ("p_v_sel", KV), ("p_k_win", KV), ("p_v_win", KV), ("p_ssm", (P, 2, NT_ST)), ("s_k_cmp", SKV), ("s_v_cmp", SKV),
       ("s_k_sel", SKV), ("s_v_sel", SKV), ("s_k_win", WKV), ("s_v_win", WKV), ("s_ssm", (P, 2, NT_ST, NB))]


def laid_out(i):
    state = lambda a: np.asarray(a)[0].reshape(NT_ST, P).T
    heads = np.asarray(i["w_in"])[0, :, :NH * HD].reshape(D, NKV, REP, HD)
    return {
        "w_in_heads": heads.transpose(0, 2, 1, 3).reshape(D, NH * HD),
        "peT_k": np.asarray(i["cmp_pe_k"])[0].T, "peT_v": np.asarray(i["cmp_pe_v"])[0].T,
        "k1T": np.asarray(i["peer_keys1"])[0].T, "k2T": np.asarray(i["peer_keys2"])[0].T,
        "log_dt": np.asarray(i["ssm_log_dt"])[0].reshape(NT_ST, P // STATE).T,
        "a_re": state(i["ssm_a_re"]), "a_im": state(i["ssm_a_im"]),
        "b_re": np.asarray(i["ssm_b_re"])[0].reshape(NT_ST, P, GRP_CH).transpose(1, 0, 2),
        "b_im": np.asarray(i["ssm_b_im"])[0].reshape(NT_ST, P, GRP_CH).transpose(1, 0, 2),
        "c_re": np.asarray(i["ssm_c_re"])[0].transpose(0, 2, 1).reshape(NT_ST, P, GRP_CH).transpose(1, 0, 2),
        "c_im": np.asarray(i["ssm_c_im"])[0].transpose(0, 2, 1).reshape(NT_ST, P, GRP_CH).transpose(1, 0, 2),
        "d_skip": np.asarray(i["ssm_d"])[0].reshape(4, P).T,
        "h0_re": np.asarray(i["state_ssm_re"])[0].reshape(NB, NT_ST, P).transpose(2, 1, 0),
        "h0_im": np.asarray(i["state_ssm_im"])[0].reshape(NB, NT_ST, P).transpose(2, 1, 0),
    }


def kernel(**inputs):
    import concourse.bacc as _bacc
    from concourse.bass_utils import run_bass_kernel_spmd as _run

    nc = _bacc.Bacc("TRN2", target_bir_lowering=False, num_devices=1)
    arrays, io = {}, {}
    given = {n: np.asarray(inputs[n]) for n in IN}
    given.update(laid_out(inputs))
    given.update(host_constants())
    for name, a in given.items():
        a = np.ascontiguousarray(a)
        arrays[f"in_{name}"] = a
        io[name] = nc.dram_tensor(f"in_{name}", a.shape, mybir.dt.from_np(a.dtype), kind="ExternalInput").ap()
    for name, shape in OUT:
        io[name] = nc.dram_tensor(f"out_{name}", shape, F32, kind="ExternalOutput").ap()
    build(nc, io)
    r = _run(nc, [arrays], core_ids=[0]).results[0]
    got = {n: r[f"out_{n}"] for n, _ in OUT}
    states = lambda a: a.T.reshape(1, 1, NT_ST * P // STATE, STATE)
    got["p_ssm_re"], got["p_ssm_im"] = states(got["p_ssm"][:, 0]), states(got["p_ssm"][:, 1])
    many = lambda a: a.transpose(2, 1, 0).reshape(1, NB, NT_ST * P // STATE, STATE)
    got["s_ssm_re"], got["s_ssm_im"] = many(got["s_ssm"][:, 0]), many(got["s_ssm"][:, 1])
    order = ["y_prompt", "y_sample", "p_k_cmp", "p_v_cmp", "p_k_sel", "p_v_sel", "p_k_win", "p_v_win", "p_ssm_re",
             "p_ssm_im", "s_k_cmp", "s_v_cmp", "s_k_sel", "s_v_sel", "s_k_win", "s_v_win", "s_ssm_re", "s_ssm_im"]
    return tuple(got[n] for n in order)
```
